# Optimizing a Trainium2 kernel written in Bass

```python
import math
import jax, jax.numpy as jnp
from jax import lax
import numpy as np

D_MODEL = 1024
BATCH = 1
SEQ = 512
DEPTH = 2

EXPAND = 2
D_INNER = EXPAND * D_MODEL
HEAD_DIM = 64
ROPE_THETA = 500000.0
ROPE_DIM = HEAD_DIM // 4
BLOCK = 128
EPS = 1e-6

DA_WIDTH = D_INNER // 2
DA_VDIM = 2 * HEAD_DIM
DA_HEADS = DA_WIDTH // DA_VDIM
HG_WIDTH = D_INNER - DA_WIDTH
HG_EXPAND = 128
HG_HEADS = HG_WIDTH // HG_EXPAND
HG_CHUNK = 64
SW_HEADS = D_INNER // HEAD_DIM
SW_KV_HEADS = SW_HEADS // 8
SW_WINDOW = 128

N_EVEN = (DEPTH + 1) // 2
N_ODD = DEPTH // 2
EVEN_SIZES = (DA_WIDTH, DA_WIDTH, DA_WIDTH, DA_WIDTH,
              HG_WIDTH, HG_WIDTH, HG_WIDTH, HG_WIDTH, HG_WIDTH)
ODD_SIZES = (D_INNER, SW_KV_HEADS * HEAD_DIM, SW_KV_HEADS * HEAD_DIM, D_INNER)
EVEN_IN = sum(EVEN_SIZES)
ODD_IN = sum(ODD_SIZES)

kernel_name = "hybrid_diffattn_hgrn2_swa_encoder"

def rmsnorm(x, w):
    xf = x.astype(jnp.float32)
    y = xf * lax.rsqrt(jnp.mean(xf * xf, axis=-1, keepdims=True) + EPS)
    return (y * w.astype(jnp.float32)).astype(x.dtype)

def split_cols(t, sizes):
    idx = [int(v) for v in np.cumsum(sizes)[:-1]]
    return jnp.split(t, idx, axis=-1)

def rope_tables(seq):
    inv = ROPE_THETA ** (-jnp.arange(0, ROPE_DIM, 2, dtype=jnp.float32) / ROPE_DIM)
    ang = jnp.arange(seq, dtype=jnp.float32)[:, None] * inv[None, :]
    return jnp.cos(ang), jnp.sin(ang)

def partial_rope(x, cos, sin):
    c = cos[None, :, None, :].astype(x.dtype)
    s = sin[None, :, None, :].astype(x.dtype)
    x1 = x[..., :ROPE_DIM // 2]
    x2 = x[..., ROPE_DIM // 2:ROPE_DIM]
    return jnp.concatenate([x1 * c - x2 * s, x2 * c + x1 * s, x[..., ROPE_DIM:]], axis=-1)

def differential_attention(q, k, v, lam_p, lam_init, subln_w, cos, sin):
    B, S, _ = q.shape
    H = DA_HEADS
    n = S // BLOCK
    q = partial_rope(q.reshape(B, S, 2 * H, HEAD_DIM), cos, sin).reshape(B, S, H, 2, HEAD_DIM)
    k = partial_rope(k.reshape(B, S, 2 * H, HEAD_DIM), cos, sin).reshape(B, S, H, 2, HEAD_DIM)
    v = v.reshape(B, S, H, DA_VDIM)
    lp = lam_p.astype(jnp.float32)
    lam = jnp.exp(jnp.sum(lp[0] * lp[1])) - jnp.exp(jnp.sum(lp[2] * lp[3])) + lam_init
    scale = HEAD_DIM ** -0.5
    qb = q.reshape(B, n, BLOCK, H, 2, HEAD_DIM).transpose(1, 0, 2, 3, 4, 5)

    def one_block(qx):
        s = jnp.einsum('bqhcd,bkhcd->bhcqk', qx, k, preferred_element_type=jnp.float32) * scale
        p = jax.nn.softmax(s, axis=-1)
        a = p[:, :, 0] - lam * p[:, :, 1]
        return jnp.einsum('bhqk,bkhv->bqhv', a.astype(v.dtype), v)

    o = lax.map(one_block, qb).transpose(1, 0, 2, 3, 4).reshape(B, S, H, DA_VDIM)
    o = rmsnorm(o, subln_w) * (1.0 - lam_init)
    return o.reshape(B, S, DA_WIDTH)

def hgrn2_chunk_scan(q, log_f, k, v):
    B, S, H, dk = q.shape
    dv = v.shape[-1]
    C = HG_CHUNK
    n = S // C

    def to_chunks(t):
        return t.reshape(B, n, C, H, t.shape[-1]).transpose(1, 0, 3, 2, 4)

    qc, gc, kc, vc = to_chunks(q), to_chunks(log_f), to_chunks(k), to_chunks(v)
    G = jnp.cumsum(gc, axis=3)
    tril = jnp.tril(jnp.ones((C, C), dtype=bool))[None, None, :, :, None]

    def step(state, xs):
        qb, Gb, kb, vb = xs
        diff = Gb[:, :, :, None, :] - Gb[:, :, None, :, :]
        decay = jnp.exp(jnp.where(tril, diff, -jnp.inf))
        A = jnp.einsum('bhtd,bhsd,bhtsd->bhts', qb, kb, decay)
        o = jnp.einsum('bhts,bhsv->bhtv', A, vb)
        o = o + jnp.einsum('bhtd,bhdv->bhtv', qb * jnp.exp(Gb), state)
        g_last = Gb[:, :, -1]
        k_dec = kb * jnp.exp(g_last[:, :, None, :] - Gb)
        new_state = jnp.exp(g_last)[..., None] * state + jnp.einsum('bhsd,bhsv->bhdv', k_dec, vb)
        return new_state, o

    s0 = jnp.zeros((B, H, dk, dv), jnp.float32)
    _, o = lax.scan(step, s0, (qc, G, kc, vc))
    return o.transpose(1, 0, 3, 2, 4).reshape(B, S, H, dv)

def hgrn2_bidirectional(q, f_fwd, f_bwd, i, lb, norm_w):
    B, S, _ = q.shape
    shp = (B, S, HG_HEADS, HG_EXPAND)
    qf = jax.nn.silu(q.astype(jnp.float32)).reshape(shp)
    vf = i.astype(jnp.float32).reshape(shp)

    def gates(z, lb_d):
        z = z.astype(jnp.float32).reshape(shp)
        lb_d = lb_d.reshape(HG_HEADS, HG_EXPAND)
        log_f = jnp.logaddexp(jnp.log(lb_d), jnp.log1p(-lb_d) + jax.nn.log_sigmoid(z))
        key = (1.0 - lb_d) * jax.nn.sigmoid(-z)
        return log_f, key

    lf_f, k_f = gates(f_fwd, lb[0])
    o_f = hgrn2_chunk_scan(qf, lf_f, k_f, vf)
    lf_b, k_b = gates(f_bwd, lb[1])
    rev = lambda t: jnp.flip(t, axis=1)
    o_b = rev(hgrn2_chunk_scan(rev(qf), rev(lf_b), rev(k_b), rev(vf)))
    o = rmsnorm(o_f + o_b, norm_w)
    return o.reshape(B, S, HG_WIDTH).astype(q.dtype)

def window_gqa_with_sink(q, k, v, sink, cos, sin):
    B, S, _ = q.shape
    Hkv = SW_KV_HEADS
    G = SW_HEADS // Hkv
    n = S // BLOCK
    q = partial_rope(q.reshape(B, S, SW_HEADS, HEAD_DIM), cos, sin)
    k = partial_rope(k.reshape(B, S, Hkv, HEAD_DIM), cos, sin)
    v = v.reshape(B, S, Hkv, HEAD_DIM)

    def banded(t):
        tp = jnp.pad(t, ((0, 0), (BLOCK, BLOCK), (0, 0), (0, 0))).reshape(B, n + 2, BLOCK, Hkv, HEAD_DIM)
        band = jnp.concatenate([tp[:, :-2], tp[:, 1:-1], tp[:, 2:]], axis=2)
        return band.transpose(1, 0, 2, 3, 4)

    qb = q.reshape(B, n, BLOCK, Hkv, G, HEAD_DIM).transpose(1, 0, 2, 3, 4, 5)
    kb, vb = banded(k), banded(v)
    sink_g = sink.astype(jnp.float32).reshape(Hkv, G)[None, :, :, None, None]
    q_idx = jnp.arange(BLOCK)[:, None]
    k_off = jnp.arange(3 * BLOCK)[None, :] - BLOCK
    in_window = jnp.abs(k_off - q_idx) <= SW_WINDOW
    scale = HEAD_DIM ** -0.5

    def one_block(args):
        blk, qx, kx, vx = args
        s = jnp.einsum('bqhgd,bkhd->bhgqk', qx, kx, preferred_element_type=jnp.float32) * scale
        key_pos = blk * BLOCK + k_off
        valid = in_window & (key_pos >= 0) & (key_pos < S)
        s = jnp.where(valid, s, -jnp.inf)
        m = jnp.maximum(jnp.max(s, axis=-1, keepdims=True), sink_g)
        p = jnp.exp(s - m)
        p = p / (jnp.sum(p, axis=-1, keepdims=True) + jnp.exp(sink_g - m))
        return jnp.einsum('bhgqk,bkhd->bqhgd', p.astype(vx.dtype), vx)

    o = lax.map(one_block, (jnp.arange(n), qb, kb, vb))
    return o.transpose(1, 0, 2, 3, 4, 5).reshape(B, S, SW_HEADS * HEAD_DIM)

def even_layer(x, norm_w, w_in, w_out, lam_p, lam_init, subln_w, hg_norm_w, lb, cos, sin):
    h = rmsnorm(x, norm_w)
    proj = jnp.einsum('bsd,de->bse', h, w_in)
    qa, ka, va, ga, qh, ffw, fbw, ih, gh = split_cols(proj, EVEN_SIZES)
    oa = differential_attention(qa, ka, va, lam_p, lam_init, subln_w, cos, sin) * jax.nn.silu(ga)
    ob = hgrn2_bidirectional(qh, ffw, fbw, ih, lb, hg_norm_w) * jax.nn.silu(gh)
    return jnp.einsum('bse,ed->bsd', jnp.concatenate([oa, ob], axis=-1), w_out)

def odd_layer(x, norm_w, w_in, w_out, sink, cos, sin):
    h = rmsnorm(x, norm_w)
    proj = jnp.einsum('bsd,de->bse', h, w_in)
    qc, kc, vc, gc = split_cols(proj, ODD_SIZES)
    oc = window_gqa_with_sink(qc, kc, vc, sink, cos, sin) * jax.nn.silu(gc)
    return jnp.einsum('bse,ed->bsd', oc, w_out)

def setup_inputs(seed: int = 0) -> dict:
    key = jax.random.key(seed)
    ks = jax.random.split(key, 16)
    f32 = jnp.float32
    nrm = lambda k, shp, sc: jax.random.normal(k, shp, f32) * sc
    return {
        "x": nrm(ks[0], (BATCH, SEQ, D_MODEL), 1.0),
        "norm_even": 1.0 + nrm(ks[1], (N_EVEN, D_MODEL), 0.02),
        "w_in_even": nrm(ks[2], (N_EVEN, D_MODEL, EVEN_IN), D_MODEL ** -0.5),
        "lambda_qk": nrm(ks[3], (N_EVEN, 4, HEAD_DIM), 0.1),
        "subln_w": 1.0 + nrm(ks[4], (N_EVEN, DA_VDIM), 0.02),
        "hgrn_norm_w": 1.0 + nrm(ks[5], (N_EVEN, HG_EXPAND), 0.02),
        "hgrn_lb_logits": nrm(ks[6], (2, N_EVEN, HG_WIDTH), 0.5),
        "w_out_even": nrm(ks[7], (N_EVEN, D_INNER, D_MODEL), D_INNER ** -0.5),
        "norm_odd": 1.0 + nrm(ks[8], (N_ODD, D_MODEL), 0.02),
        "w_in_odd": nrm(ks[9], (N_ODD, D_MODEL, ODD_IN), D_MODEL ** -0.5),
        "sink_logits": nrm(ks[10], (N_ODD, SW_HEADS), 0.5),
        "w_out_odd": nrm(ks[11], (N_ODD, D_INNER, D_MODEL), D_INNER ** -0.5),
        "final_norm": 1.0 + nrm(ks[12], (D_MODEL,), 0.02),
    }

def reference(x, norm_even, w_in_even, lambda_qk, subln_w, hgrn_norm_w, hgrn_lb_logits,
              w_out_even, norm_odd, w_in_odd, sink_logits, w_out_odd, final_norm):
    S = x.shape[1]
    cos, sin = rope_tables(S)
    lb_cum = jnp.cumsum(jax.nn.softmax(hgrn_lb_logits.astype(jnp.float32), axis=1), axis=1)
    lb_all = lb_cum - lb_cum[:, :1]
    for layer in range(DEPTH):
        j = layer // 2
        if layer % 2 == 0:
            lam_init = 0.8 - 0.6 * math.exp(-0.3 * layer)
            x = x + even_layer(x, norm_even[j], w_in_even[j], w_out_even[j], lambda_qk[j],
                               lam_init, subln_w[j], hgrn_norm_w[j], lb_all[:, j], cos, sin)
        else:
            x = x + odd_layer(x, norm_odd[j], w_in_odd[j], w_out_odd[j], sink_logits[j], cos, sin)
    return rmsnorm(x, final_norm)


_drawn_inputs = setup_inputs


def setup_inputs(seed=0):
    import zlib

    import numpy as np

    out = dict(_drawn_inputs(seed))
    spreads = {}
    factors = {'norm_even': 3.165,
     'lambda_qk': 8.0,
     'subln_w': 8.0,
     'hgrn_norm_w': 6.455,
     'norm_odd': 8.0,
     'sink_logits': 8.0,
     'final_norm': 2.893}
    for name, (base, spread) in spreads.items():
        noise = np.random.default_rng([zlib.crc32(name.encode()), seed]).standard_normal(out[name].shape)
        drawn = base * np.exp(spread * noise) if base else spread * noise
        out[name] = __import__('jax').numpy.asarray(drawn.astype(out[name].dtype))
    for name, factor in factors.items():
        out[name] = (out[name] * factor).astype(out[name].dtype)
    return out
```

```python
from contextlib import ExitStack

import numpy as np

import concourse.bass as bass
from concourse import mybir

ALU = mybir.AluOpType
ACT = mybir.ActivationFunctionType
AX_X = mybir.AxisListType.X
F32 = mybir.dt.float32
F32R = mybir.dt.float32r
BF16 = mybir.dt.bfloat16
U8 = mybir.dt.uint8

P = 128
SEQ = 512
DM = 1024
KT = DM // P
DI = 2 * DM
HD = 64
ROPE = HD // 4
NC = SEQ // P
HEADS = 8
PAIRS = 16
LEVELS = 7
LP = P + 1
SCALE = HD ** -0.5
LAM_INIT = 0.8 - 0.6 * 1.0
EPS = 1e-6
MASKED = -1e30
DMA = 16
SWAP = list(range(ROPE // 2, ROPE)) + list(range(ROPE // 2)) + list(range(ROPE, 32))


class Count:

    def __init__(self, sem, per=0, lead=0, unit=1):
        self.sem, self.per, self.lead, self.unit = sem, per, lead, unit

    def at(self, h, n):
        return self.unit * (self.lead + self.per * h + n)

    def due(self, h, n):
        return not isinstance(self.at(h, n), int) or self.at(h, n) > 0


def chunked(ap, width=P):
    return ap.rearrange("p (c w) -> p c w", w=width)


class Bank:

    def __init__(self, nc, ctx, name, per=0, lead=0):
        self.t = ctx.enter_context(nc.psum_tensor(f"bank_{name}", [P, SEQ], F32))
        self.full = Count(ctx.enter_context(nc.semaphore(f"{name}_full")), per, lead)
        self.free = Count(ctx.enter_context(nc.semaphore(f"{name}_free")), per, lead)

    def __getitem__(self, at):
        return self.t[at]


def split_product(pe, out, hi, lo, moving_hi, moving_lo, start, stop):
    pe.matmul(out, hi, moving_hi, start=start, stop=False)
    pe.matmul(out, hi, moving_lo, start=False, stop=False)
    return pe.matmul(out, lo, moving_hi, start=False, stop=stop)


class Norm:

    def __init__(self, nc, ctx, name, xT, w, ones, eps, tmp, scaled, rstd, bank, hH=None, hL=None):
        sem = lambda s: Count(ctx.enter_context(nc.semaphore(f"{name}_{s}")))
        self.squared, self.summed, self.logged, self.rooted = map(sem, ("squared", "summed", "logged", "rooted"))
        self.scaled_to, self.high, self.low = map(sem, ("scaled", "high", "low"))
        self.xT, self.w, self.ones, self.eps, self.tmp, self.scaled = xT, w, ones, eps, tmp, scaled
        self.rstd, self.bank, self.hH, self.hL = rstd, bank, hH, hL

    def act(self, act):
        for k in range(KT):
            if self.summed.due(0, k - 1):
                act.wait_ge(self.summed.sem, self.summed.at(0, k - 1))
            act.activation(self.tmp[:, k % 2], self.xT[:, k], ACT.Square).then_inc(self.squared.sem, 1)
        act.wait_ge(self.summed.sem, self.summed.at(0, KT))
        act.activation(self.rstd, self.bank[:], ACT.Ln, bias=self.eps, scale=1.0 / DM).then_inc(self.logged.sem, 1)
        act.wait_ge(self.logged.sem, self.logged.at(0, 1))
        act.activation(self.rstd, self.rstd, ACT.Exp, scale=-0.5).then_inc(self.rooted.sem, 1)
        if self.hH is not None:
            for k in range(KT):
                act.wait_ge(self.scaled_to.sem, self.scaled_to.at(0, k + 1))
                act.activation(self.hH[:, k], self.scaled[:, k % 2], ACT.Copy).then_inc(self.high.sem, 1)

    def pe(self, pe):
        for k in range(KT):
            pe.wait_ge(self.squared.sem, self.squared.at(0, k + 1))
            pe.matmul(self.bank[:], self.ones, self.tmp[:, k % 2], start=k == 0,
                      stop=k == KT - 1).then_inc(self.summed.sem, 1)

    def dve(self, dve, out=None):
        dve.wait_ge(self.rooted.sem, self.rooted.at(0, 1))
        for k in range(KT):
            if out is None:
                if k >= 2:
                    dve.wait_ge(self.high.sem, self.high.at(0, k - 1))
                    dve.wait_ge(self.low.sem, self.low.at(0, k - 1))
                to = self.scaled[:, k % 2]
            else:
                to = out[:, k]
            dve.scalar_tensor_tensor(out=to, in0=self.xT[:, k], scalar=self.w[:, k:k + 1], in1=self.rstd,
                                     op0=ALU.mult, op1=ALU.mult).then_inc(self.scaled_to.sem, 1)
            if out is None and k:
                self.lows(dve, k - 1)
        if out is None:
            self.lows(dve, KT - 1)

    def lows(self, dve, k):
        dve.wait_ge(self.high.sem, self.high.at(0, k + 1))
        dve.wait_ge(self.scaled_to.sem, self.scaled_to.at(0, k + 1))
        dve.tensor_tensor(self.hL[:, k], self.scaled[:, k % 2], self.hH[:, k].bitcast(F32),
                          ALU.subtract).then_inc(self.low.sem, 1)


def even_layer(nc, xT, eye, ones, rope, eps, x, w_in, w_out, norm, lam, subln, hgw, rope_d, levels_d, eye_d):
    with ExitStack() as ctx:
        sb = lambda name, shape, dt=F32: ctx.enter_context(nc.sbuf_tensor(name, shape, dt))
        sem = lambda name, *a, **k: Count(ctx.enter_context(nc.semaphore(name)), *a, **k)

        hH, hL = sb("hH", [P, KT, SEQ], F32R), sb("hL", [P, KT, SEQ], F32R)
        w_raw = sb("w_raw", [P, 3, KT, P])
        w_hi, w_lo = sb("w_hi", [P, 3, KT, P], F32R), sb("w_lo", [P, 3, KT, P], F32R)
        o_raw = sb("o_raw", [P, DM])
        o_hi, o_lo = sb("o_hi", [P, 2, DM], F32R), sb("o_lo", [P, 2, DM], F32R)
        y = sb("y", [P, 2, 2, SEQ], F32R)
        parts = sb("parts", [P, 2, SEQ], F32R)
        qs = sb("qs", [P, 2, SEQ], F32R)
        ks = sb("ks", [P, 2, 2, SEQ], F32R)
        v = sb("v", [P, NC, P])
        probs = sb("probs", [P, 2, SEQ])
        mix = sb("mix", [P, SEQ])
        mixT = sb("mixT", [P, NC, SEQ])
        gate_a = sb("gate_a", [P, SEQ])
        vt = sb("vt", [P, SEQ])
        turned = sb("turned", [P, 2, SEQ])
        small = sb("small", [P, 64])
        gf, gb = sb("gf", [P, NC, LP]), sb("gb", [P, NC, LP])
        lf = sb("lf", [P, SEQ])
        keys = sb("keys", [P, 2, SEQ])
        query = sb("query", [P, SEQ])
        gate_h = sb("gate_h", [P, SEQ])
        vh = sb("vh", [P, NC, P])
        soft = sb("soft", [P, 2, SEQ])
        decay = sb("decay", [P, 2, SEQ])
        scaled = sb("scaled", [P, 2, 2, SEQ])
        attT = sb("attT", [P, 2560])
        sq, rstd, yn = sb("sq", [P, SEQ]), sb("rstd", [P, SEQ]), sb("yn", [P, SEQ])
        level_mask = sb("level_mask", [P, LEVELS, P], U8)
        wn = sb("wn", [P, KT])
        w_sub, w_hg = sb("w_sub", [P, 1]), sb("w_hg", [P, 1])

        row_max, neg_max = small[:, 0:8], small[:, 8:16]
        row_sum, weight = small[:, 16:24], small[:, 24:32]
        lam_t, lam_e = small[:, 32:33], small[:, 34:36]
        total = small[:, 40:48].rearrange("p (d c) -> p d c", d=2)
        att = attT[:, 0:NC * SEQ].rearrange("p (s t) -> p s t", s=NC)
        att_diag = attT[:, :].rearrange("p (c w) -> p c w", w=SEQ + P)[:, :, 0:P]
        key_sum = attT[:, NC * SEQ:2560]
        mask_raw = scaled[:, :, :, :].rearrange("p a b t -> p (a b t)")[:, 0:LEVELS * P].rearrange(
            "p (l t) -> p l t", t=P)

        PB = [Bank(nc, ctx, f"proj{b}", 3, 1) for b in range(3)]
        S = [Bank(nc, ctx, "score0", 10, 0), Bank(nc, ctx, "score1", 9, 0)]
        O, W = Bank(nc, ctx, "out", 6, -4), Bank(nc, ctx, "wide", 4, -3)
        T = Bank(nc, ctx, "turn", 8, 0)

        x_landed, landed = sem("x_landed", unit=DMA), sem("constants_landed", unit=DMA)
        x_turned, x_kept = sem("x_turned"), sem("x_kept")
        ready = sem("constants_ready")
        lam_steps = sem("lambda_steps")
        w_in_sem = [sem(f"weights{i}_landed", 3, 1, unit=DMA) for i in range(3)]
        w_high, w_low = sem("weights_high", 9, 3), sem("weights_low", 9, 3)
        o_in = sem("out_weights_landed", 2, 0, unit=DMA)
        o_high, o_low = sem("out_weights_high", 2), sem("out_weights_low", 2)
        softplus = sem("softplus", 6)
        log_f = sem("log_forget", 2)
        summed = sem("decays_summed", 2 * NC)
        key_exp = sem("keys_ready", 2)
        peak, neg_peak = sem("row_max", 8), sem("neg_row_max", 4)
        mixing = sem("mixing", 16)
        roped = sem("roped", 10, 5 * 2)
        q_moved, k_moved = sem("q_moved", 4, 4, unit=DMA), sem("k_moved", 4, 4, unit=DMA)
        squared = sem("squared", 2, -1)
        rooted = sem("rooted", 2, -1)
        y_hg, y_da = sem("y_recurrence", 3, -3), sem("y_attention", 3)
        key_both = sem("key_sum", 1)
        far_diff, far_exp = sem("far_differences", 2), sem("far_decays", 5)
        far_scaled = sem("far_scaled", 10)
        far_kept = sem("far_kept", 3)
        near_fwd, near_bwd = sem("near_differences_fwd", 2 * LEVELS), sem("near_differences_bwd", 2 * LEVELS)
        place_go = sem("place_go")
        load_go = sem("load_go")
        near_exp, near_scaled = sem("near_decays", LEVELS), sem("near_scaled", 3 * LEVELS)
        nrm = Norm(nc, ctx, "norm_even", xT, wn, ones, eps, turned, soft, rstd[:], O, hH, hL)

        w_cols = w_in.rearrange("(k p) n -> p k n", p=P)
        SECTION = {1: 5, 2: 6, 3: 7, 4: 4, 5: 8, 6: 3, 7: 0, 8: 1, 9: 2}

        def bank_of(n):
            return PB[(n - 1) % 3], (n - 1) // 3 + 1

        def near(ap, l, first=0):
            b = 1 << l
            if len(ap.shape) == 3:
                g = ap[:, :, first:first + P].rearrange("p c (n h b) -> p c n h b", h=2, b=b)
                return g[:, :, :, 0, :], g[:, :, :, 1, :]
            g = ap.rearrange("p (c n h b) -> p c n h b", c=NC, h=2, b=b)
            return g[:, :, :, 0, :], g[:, :, :, 1, :]

        def middle(ap, l):
            b = 1 << l
            g = ap[:, :, 0:P].rearrange("p c (n w) -> p c n w", w=2 * b)[:, :, :, b:b + 1]
            return g.broadcast_to([P, NC, P // (2 * b), b])

        def buf(l):
            return decay if l % 2 == 0 else soft

        block = ctx.enter_context(nc.Block())

        @block.sync
        def _(sp):
            tiles = (mixT[:, :, :].rearrange("p c t -> p (c t)"), attT[:, 0:2 * DM])
            for t in range(NC):
                sp.dma_start(tiles[t // 2][:, (t % 2) * DM:(t % 2 + 1) * DM],
                             x[t * P:(t + 1) * P, :]).then_inc(x_landed.sem, DMA)
            sp.dma_start(eye[:], eye_d).then_inc(x_landed.sem, DMA)
            for to, of in ((wn[:], norm), (w_sub[:], subln), (w_hg[:], hgw), (rope[:], rope_d), (mask_raw, levels_d)):
                sp.dma_start(to, of).then_inc(landed.sem, DMA)
            sp.dma_start(yn[:, 0:4 * HD], lam.broadcast_to([P, 4 * HD])).then_inc(landed.sem, DMA)

            def load(h, n):
                if w_low.due(h, n - 3):
                    sp.wait_ge(w_low.sem, w_low.at(h, n - 3))
                sp.sem_inc(load_go.sem, 1)
                head = h + 1 if n > 6 else h
                col = SECTION[(n - 1) % 9 + 1] * DM + head * P
                s = (n + 2) % 3
                sp.dma_start(w_raw[:, s], w_cols[:, :, bass.ds(col, P)]).then_inc(w_in_sem[s].sem, DMA)

            def load_out(h, m):
                if o_low.due(h, m):
                    sp.wait_ge(o_low.sem, o_low.at(h, m))
                sp.sem_inc(load_go.sem, 1)
                row = m * DM + h * P
                sp.dma_start(o_raw[:], w_out[bass.ds(row, P), :]).then_inc(o_in.sem, DMA)

            def move_q(h):
                sp.wait_ge(roped.sem, roped.at(h, 5))
                if S[1].full.due(h, 4):
                    sp.wait_ge(S[1].full.sem, S[1].full.at(h, 4))
                for c in range(2):
                    for part in range(2):
                        sp.dma_start(qs[HD * part:HD * part + HD, c, :].bitcast(F32),
                                     parts[HD * c:HD * c + HD, part, :].bitcast(F32)).then_inc(q_moved.sem, DMA)

            def move_k(h):
                sp.wait_ge(roped.sem, roped.at(h, 10))
                for c in range(2):
                    for twice in range(2):
                        sp.dma_start(ks[HD * twice:HD * twice + HD, c, :, :].bitcast(F32),
                                     parts[HD * c:HD * c + HD, :, :].bitcast(F32)).then_inc(k_moved.sem, DMA)

            for n in (-2, -1, 0):
                load(0, n)
            for n in (1, 2, 3):
                load(0, n)
            move_q(-1)
            move_k(-1)

            def iteration(h, last):
                for n in range(4, 7):
                    load(h, n)
                load_out(h, 0)
                if not last:
                    for n in range(7, 12):
                        load(h, n)
                load_out(h, 1)
                if not last:
                    load(h, 12)
                    move_q(h)
                    move_k(h)

            iteration(0, False)
            with sp.Fori(1, HEADS - 1) as h:
                iteration(h, False)
            iteration(HEADS - 1, True)

        @block.tensor
        def _(pe):
            pe.sem_inc(O.full.sem, 1)
            pe.sem_inc(W.full.sem, 1)
            pe.wait_ge(x_landed.sem, x_landed.at(0, 5))
            tiles = (mixT[:, :, :].rearrange("p c t -> p (c t)"), attT[:, 0:2 * DM])
            for k in range(KT):
                if x_kept.due(0, k - 1):
                    pe.wait_ge(x_kept.sem, x_kept.at(0, k - 1))
                for t in range(NC):
                    mm = pe.transpose(S[k % 2][:, t * P:(t + 1) * P],
                                      tiles[t // 2][:, (t % 2) * DM + k * P:(t % 2) * DM + (k + 1) * P], eye[:])
                mm.then_inc(x_turned.sem, 1)
            pe.wait_ge(ready.sem, ready.at(0, 4))
            nrm.pe(pe)

            def proj(h, n):
                bank, use = bank_of(n)
                pe.wait_ge(w_low.sem, w_low.at(h, n))
                if bank.free.due(h, use - 1):
                    pe.wait_ge(bank.free.sem, bank.free.at(h, use - 1))
                s = (n + 2) % 3
                for k in range(KT):
                    mm = split_product(pe, bank[:], w_hi[:, s, k], w_lo[:, s, k], hH[:, k], hL[:, k],
                                       k == 0, k == KT - 1)
                mm.then_inc(bank.full.sem, 1)

            def turn(h, use, of):
                if T.free.due(h, use - 1):
                    pe.wait_ge(T.free.sem, T.free.at(h, use - 1))
                for c in range(NC):
                    mm = pe.transpose(T[:, c * P:(c + 1) * P], of[:, c * P:(c + 1) * P], eye[:])
                mm.then_inc(T.full.sem, 1)

            def scores(h, t):
                if t == 0:
                    pe.wait_ge(q_moved.sem, q_moved.at(h, 0))
                    pe.wait_ge(k_moved.sem, k_moved.at(h, 0))
                for c in range(2):
                    if S[c].free.due(h, t):
                        pe.wait_ge(S[c].free.sem, S[c].free.at(h, t))
                    pe.matmul(S[c][:], qs[:, c, t * P:(t + 1) * P], ks[:, c, 0, :], start=True, stop=False)
                    pe.matmul(S[c][:], qs[:, c, t * P:(t + 1) * P], ks[:, c, 1, :], start=False,
                              stop=True).then_inc(S[c].full.sem, 1)

            def turn_mix(h, t):
                pe.wait_ge(mixing.sem, mixing.at(h, 4 * (t + 1)))
                turn(h, 3 + t, mix)

            def values(h, use, vals, probsT):
                if O.free.due(h, use - 1):
                    pe.wait_ge(O.free.sem, O.free.at(h, use - 1))
                for c in range(NC):
                    mm = pe.matmul(O[:], vals[:, c, :], probsT[:, c, :], start=c == 0, stop=c == NC - 1)
                mm.then_inc(O.full.sem, 1)

            def sum_squares(h, use, n):
                pe.wait_ge(T.free.sem, T.free.at(h, use - 1))
                pe.wait_ge(squared.sem, squared.at(h, n))
                pe.matmul(T[:], ones, sq[:], start=True, stop=True).then_inc(T.full.sem, 1)

            def out_tiles(h, js):
                pe.wait_ge(y_hg.sem, y_hg.at(h, 3))
                pe.wait_ge(y_da.sem, y_da.at(h, 0))
                pe.wait_ge(o_low.sem, o_low.at(h, 0))
                for j in js:
                    bank, use = (W, j // 2 + 1) if j % 2 == 0 else (O, j // 2 + 2)
                    pe.wait_ge(bank.free.sem, bank.free.at(h, use - 1))
                    for m in range(2):
                        mm = split_product(pe, bank[:], o_hi[:, m, j * P:(j + 1) * P], o_lo[:, m, j * P:(j + 1) * P],
                                           y[:, m, 0], y[:, m, 1], m == 0, m == 1)
                    mm.then_inc(bank.full.sem, 1)

            def diagonal(h):
                pe.wait_ge(key_both.sem, key_both.at(h, 1))
                pe.wait_ge(PB[0].free.sem, PB[0].free.at(h, 2))
                pe.wait_ge(S[0].free.sem, S[0].free.at(h, 4))
                for c in range(NC):
                    mm = pe.matmul(S[0][:, c * P:(c + 1) * P], key_sum[:, c * P:(c + 1) * P],
                                   query[:, c * P:(c + 1) * P], start=True, stop=True)
                mm.then_inc(S[0].full.sem, 1)

            def far(h, x):
                qf, kf, qb, kb = (scaled[:, 0, 0], scaled[:, 0, 1], scaled[:, 1, 0], scaled[:, 1, 1])
                at = lambda a, i, w=1: a[:, i * P:(i + w) * P]
                jobs = {1: (S[1], 5, [(0, at(kf, 0), at(qf, 0)), (1, at(kf, 3), at(qf, 1, 2)), (3, at(kf, 2), at(qf, 3))]),
                        2: (S[0], 6, [(0, at(kf, 1), at(qf, 1, 2)), (2, at(kb, 1), at(qb, 0, 2))]),
                        3: (S[1], 6, [(0, at(kb, 3), at(qb, 0, 2)), (2, at(kb, 2), at(qb, 2)), (3, at(kb, 0), at(qb, 3))])}
                bank, use, products = jobs[x]
                pe.wait_ge(far_scaled.sem, far_scaled.at(h, 10))
                pe.wait_ge(bank.free.sem, bank.free.at(h, use - 1))
                for col, key, qry in products:
                    mm = pe.matmul(bank[:, col * P:col * P + qry.shape[1]], key, qry, start=True, stop=True)
                mm.then_inc(bank.full.sem, 1)

            def near_level(h, l):
                pe.wait_ge(near_scaled.sem, near_scaled.at(h, 3 * (l + 1)))
                pe.wait_ge(S[l % 2].free.sem, S[l % 2].free.at(h, 7 + l // 2 - 1))
                for c in range(NC):
                    mm = pe.matmul(S[l % 2][:, c * P:(c + 1) * P], scaled[:, l % 2, 0, c * P:(c + 1) * P],
                                   scaled[:, l % 2, 1, c * P:(c + 1) * P], start=True, stop=True)
                mm.then_inc(S[l % 2].full.sem, 1)

            def recurrence_values(h):
                pe.wait_ge(S[0].free.sem, S[0].free.at(h, 0))
                pe.wait_ge(S[1].free.sem, S[1].free.at(h, 0))
                pe.wait_ge(far_kept.sem, far_kept.at(h, 0))
                pe.wait_ge(T.free.sem, T.free.at(h, -6))
                values(h, 1, vh, att)

            pe.wait_ge(nrm.low.sem, nrm.low.at(0, KT))
            for n in (-2, -1, 0):
                proj(0, n)
            pe.wait_ge(PB[2].free.sem, PB[2].free.at(0, 0))
            turn(0, 1, vt)

            def iteration(h, first, last):
                proj(h, 1)
                proj(h, 2)
                if not first:
                    recurrence_values(h)
                scores(h, 0)
                proj(h, 3)
                if not first:
                    sum_squares(h, 1, 1)
                scores(h, 1)
                proj(h, 4)
                pe.wait_ge(PB[2].free.sem, PB[2].free.at(h, 1))
                turn(h, 2, vt)
                turn_mix(h, 0)
                scores(h, 2)
                proj(h, 5)
                turn_mix(h, 1)
                scores(h, 3)
                if not first:
                    out_tiles(h, range(0, 4))
                turn_mix(h, 2)
                proj(h, 6)
                turn_mix(h, 3)
                if not first:
                    out_tiles(h, range(4, 8))
                diagonal(h)
                pe.wait_ge(T.free.sem, T.free.at(h, 6))
                values(h, 6, v, mixT)
                if not last:
                    proj(h, 7)
                sum_squares(h, 7, 2)
                far(h, 1)
                far(h, 2)
                far(h, 3)
                if not last:
                    proj(h, 8)
                near_level(h, 0)
                near_level(h, 1)
                near_level(h, 2)
                if not last:
                    proj(h, 9)
                near_level(h, 3)
                near_level(h, 4)
                if not last:
                    pe.wait_ge(PB[2].free.sem, PB[2].free.at(h, 3))
                    turn(h, 8, vt)
                near_level(h, 5)
                near_level(h, 6)

            iteration(0, True, False)
            with pe.Fori(1, HEADS - 1) as h:
                iteration(h, False, False)
            iteration(HEADS - 1, False, True)
            recurrence_values(HEADS)
            sum_squares(HEADS, 0, 1)
            out_tiles(HEADS, range(8))

        @block.scalar
        def _(act):
            for k in range(KT):
                act.wait_ge(x_turned.sem, x_turned.at(0, k + 1))
                act.activation(xT[:, k], S[k % 2][:], ACT.Copy).then_inc(x_kept.sem, 1)
            act.wait_ge(ready.sem, ready.at(0, 4))
            act.wait_ge(x_kept.sem, x_kept.at(0, KT))
            act.wait_ge(lam_steps.sem, lam_steps.at(0, 2))
            act.activation(lam_e, lam_e, ACT.Exp).then_inc(lam_steps.sem, 1)

            def high(h, n):
                s = (n + 2) % 3
                act.wait_ge(w_in_sem[s].sem, w_in_sem[s].at(h, (n + 2) // 3))
                bank, use = bank_of(n - 3)
                if bank.full.due(h, use):
                    act.wait_ge(bank.full.sem, bank.full.at(h, use))
                act.activation(w_hi[:, s], w_raw[:, s], ACT.Copy).then_inc(w_high.sem, 1)

            def high_out(h, m):
                act.wait_ge(o_in.sem, o_in.at(h, m + 1))
                if O.full.due(h, 5):
                    act.wait_ge(O.full.sem, O.full.at(h, 5))
                act.activation(o_hi[:, m], o_raw[:], ACT.Copy).then_inc(o_high.sem, 1)

            def soften(h, d):
                bank = PB[d]
                at = soft[:, d]
                act.wait_ge(bank.full.sem, bank.full.at(h, 1))
                if near_scaled.due(h, 0):
                    act.wait_ge(near_scaled.sem, near_scaled.at(h, 0))
                act.activation(at, bank[:], ACT.Abs).then_inc(softplus.sem, 1)
                act.wait_ge(softplus.sem, softplus.at(h, 3 * d + 1))
                act.activation(at, at, ACT.Exp, scale=-1.0).then_inc(softplus.sem, 1)
                act.wait_ge(softplus.sem, softplus.at(h, 3 * d + 2))
                act.activation(at, at, ACT.Ln, bias=1.0).then_inc(softplus.sem, 1)

            def square(h, use, n):
                act.wait_ge(O.full.sem, O.full.at(h, use))
                act.wait_ge(T.full.sem, T.full.at(h, 7 - 8 if n == 1 else 1))
                if squared.due(h, n - 1):
                    act.wait_ge(squared.sem, squared.at(h, n - 1))
                act.activation(sq[:], O[:], ACT.Square).then_inc(squared.sem, 1)

            def root(h, use, n):
                act.wait_ge(T.full.sem, T.full.at(h, use))
                if (y_da if n == 1 else y_hg).due(h, 0 if n == 1 else 1):
                    act.wait_ge((y_da if n == 1 else y_hg).sem, (y_da if n == 1 else y_hg).at(h, 0 if n == 1 else 1))
                act.activation(rstd[:], T[:], ACT.Ln, bias=eps, scale=1.0 / P).then_inc(T.free.sem, 1)
                act.wait_ge(T.free.sem, T.free.at(h, use))
                act.activation(rstd[:], rstd[:], ACT.Exp, scale=-0.5).then_inc(rooted.sem, 1)

            def key(h, d):
                act.wait_ge(PB[d].free.sem, PB[d].free.at(h, 1))
                act.activation(keys[:, d], keys[:, d], ACT.Exp).then_inc(key_exp.sem, 1)

            def soft_max(h, t):
                act.wait_ge(neg_peak.sem, neg_peak.at(h, t + 1))
                if mixing.due(h, 4 * t):
                    act.wait_ge(mixing.sem, mixing.at(h, 4 * t))
                for c in range(2):
                    i = 2 * t + c
                    act.activation(probs[:, c], S[c][:], ACT.Exp, bias=neg_max[:, i:i + 1], scale=SCALE,
                                   accum_out=row_sum[:, i:i + 1]).then_inc(S[c].free.sem, 1)

            def keep_values(h, use, into, out_use):
                act.wait_ge(T.full.sem, T.full.at(h, use))
                if O.full.due(h, out_use):
                    act.wait_ge(O.full.sem, O.full.at(h, out_use))
                act.activation(into[:, :, :].rearrange("p c f -> p (c f)"), T[:], ACT.Copy).then_inc(T.free.sem, 1)

            def keep_mix(h, t):
                act.wait_ge(T.full.sem, T.full.at(h, 3 + t))
                if O.full.due(h, 0):
                    act.wait_ge(O.full.sem, O.full.at(h, 0))
                act.activation(mixT[:, :, t * P:(t + 1) * P], chunked(T[:]), ACT.Copy).then_inc(T.free.sem, 1)

            def silu(h, n, into):
                bank, use = bank_of(n)
                act.wait_ge(bank.full.sem, bank.full.at(h, use))
                act.activation(into[:], bank[:], ACT.Silu).then_inc(bank.free.sem, 1)

            def far_decays(h):
                act.wait_ge(summed.sem, summed.at(h, 2 * NC))
                if far_scaled.due(h, 0):
                    act.wait_ge(far_scaled.sem, far_scaled.at(h, 0))
                act.activation(total[:, 0], gf[:, :, P], ACT.Exp).then_inc(far_exp.sem, 1)
                act.activation(total[:, 1], gb[:, :, P], ACT.Exp).then_inc(far_exp.sem, 1)
                act.wait_ge(log_f.sem, log_f.at(h, 2))
                act.activation(chunked(soft[:, 0, 0:3 * P]), gf[:, 1:NC, 1:LP], ACT.Exp).then_inc(far_exp.sem, 1)
                act.activation(chunked(soft[:, 1, 0:3 * P]), gb[:, 1:NC, 0:P], ACT.Exp).then_inc(far_exp.sem, 1)
                act.wait_ge(far_diff.sem, far_diff.at(h, 2))
                flat = decay[:, :, :].rearrange("p a t -> p (a t)")[:, 0:6 * P]
                act.activation(flat, flat, ACT.Exp).then_inc(far_exp.sem, 1)

            def keep_far(h, x):
                if x == 1:
                    if O.full.due(h, 1):
                        act.wait_ge(O.full.sem, O.full.at(h, 1))
                jobs = {1: (S[1], 5, (0, 1, 4, 0), (2, 3, 4, 3)),
                        2: (S[0], 6, (1, 2, 4, 0), (2, 0, 2, 2)),
                        3: (S[1], 6, (3, 0, 3, 0), (1, 0, 1, 3))}
                bank, use, one, two = jobs[x]
                act.wait_ge(bank.full.sem, bank.full.at(h, use))
                for (s, t0, t1, col), count in ((one, far_kept), (two, bank.free)):
                    act.activation(att[:, s, t0 * P:t1 * P], bank[:, col * P:(col + t1 - t0) * P],
                                   ACT.Copy).then_inc(count.sem, 1)

            def near_decays(h, l):
                act.wait_ge(near_fwd.sem, near_fwd.at(h, 2 * (l + 1)))
                act.wait_ge(near_bwd.sem, near_bwd.at(h, 2 * (l + 1)))
                flat = buf(l)[:, :, :].rearrange("p a t -> p (a t)")
                act.activation(flat, flat, ACT.Exp).then_inc(near_exp.sem, 1)

            def keep_vt(h, n, turned_use):
                bank, use = bank_of(n)
                act.wait_ge(bank.full.sem, bank.full.at(h, use))
                if T.full.due(h, turned_use):
                    act.wait_ge(T.full.sem, T.full.at(h, turned_use))
                act.activation(vt[:], bank[:], ACT.Copy).then_inc(bank.free.sem, 1)

            nrm.act(act)
            for n in (-2, -1, 0, 1, 2):
                high(0, n)
            keep_vt(0, 0, 0)
            act.wait_ge(T.full.sem, T.full.at(0, 1))
            act.activation(v[:, :, :].rearrange("p c f -> p (c f)"), T[:], ACT.Copy).then_inc(T.free.sem, 1)

            def iteration(h, first, last):
                high(h, 3)
                soften(h, 0)
                high(h, 4)
                soften(h, 1)
                if not first:
                    square(h, 1, 1)
                key(h, 0)
                soft_max(h, 0)
                high(h, 5)
                key(h, 1)
                if not first:
                    root(h, 1, 1)
                keep_vt(h, 3, 1 if first else 0)
                soft_max(h, 1)
                high(h, 6)
                keep_values(h, 2, vh, 1)
                keep_mix(h, 0)
                soft_max(h, 2)
                if not last:
                    high(h, 7)
                keep_mix(h, 1)
                soft_max(h, 3)
                if not last:
                    high(h, 8)
                silu(h, 4, query)
                silu(h, 5, gate_h)
                keep_mix(h, 2)
                silu(h, 6, gate_a)
                keep_mix(h, 3)
                far_decays(h)
                high_out(h, 0)
                if not last:
                    high(h, 9)
                square(h, 6, 2)
                keep_far(h, 1)
                root(h, 7, 2)
                keep_far(h, 2)
                keep_far(h, 3)
                if not last:
                    high(h, 10)
                near_decays(h, 0)
                near_decays(h, 1)
                near_decays(h, 2)
                if not last:
                    high(h, 11)
                high_out(h, 1)
                near_decays(h, 3)
                near_decays(h, 4)
                if not last:
                    keep_vt(h, 9, 2)
                near_decays(h, 5)
                near_decays(h, 6)
                if not last:
                    keep_values(h, 8, v, 6)

            iteration(0, True, False)
            with act.Fori(1, HEADS - 1) as h:
                iteration(h, False, False)
            iteration(HEADS - 1, False, True)
            square(HEADS, 1, 1)
            root(HEADS, 0, 1)

        @block.vector
        def _(dve):
            dve.sem_inc(O.free.sem, 1)
            dve.sem_inc(W.free.sem, 1)
            for at, value in ((ones, 1.0), (eps, EPS), (gf[:, :, 0:1], 0.0), (gb[:, :, 0:1], 0.0)):
                dve.memset(at, value).then_inc(ready.sem, 1)
            dve.wait_ge(landed.sem, landed.at(0, 6))
            dve.tensor_copy(level_mask[:], mask_raw).then_inc(ready.sem, 1)
            pairs = yn[:, 0:4 * HD].rearrange("p (a c d) -> p a c d", a=2, c=2)
            prod = yn[:, 4 * HD:6 * HD].rearrange("p (a d) -> p a d", a=2)
            dve.tensor_tensor(prod, pairs[:, :, 0, :], pairs[:, :, 1, :], ALU.mult).then_inc(lam_steps.sem, 1)
            dve.wait_ge(lam_steps.sem, lam_steps.at(0, 1))
            dve.tensor_reduce(lam_e, prod, AX_X, ALU.add).then_inc(lam_steps.sem, 1)
            dve.wait_ge(lam_steps.sem, lam_steps.at(0, 3))
            dve.tensor_tensor(lam_t, lam_e[:, 0:1], lam_e[:, 1:2], ALU.subtract).then_inc(lam_steps.sem, 1)
            dve.wait_ge(lam_steps.sem, lam_steps.at(0, 4))
            dve.tensor_scalar(lam_t, lam_t, LAM_INIT, None, ALU.add).then_inc(lam_steps.sem, 1)
            dve.wait_ge(lam_steps.sem, lam_steps.at(0, 5))
            dve.wait_ge(ready.sem, ready.at(0, 5))
            nrm.dve(dve)

            def gates(h, d):
                bank, g = PB[d], (gf, gb)[d]
                dve.wait_ge(softplus.sem, softplus.at(h, 3 * d + 3))
                if summed.due(h, NC * d):
                    dve.wait_ge(summed.sem, summed.at(h, NC * d))
                dve.scalar_tensor_tensor(out=lf[:], in0=bank[:], scalar=0.0, in1=soft[:, d], op0=ALU.min,
                                         op1=ALU.subtract).then_inc(log_f.sem, 1)
                dve.wait_ge(log_f.sem, log_f.at(h, d + 1))
                if near_scaled.due(h, 0):
                    dve.wait_ge(near_scaled.sem, near_scaled.at(h, 0))
                dve.tensor_tensor(keys[:, d], lf[:], bank[:], ALU.subtract).then_inc(bank.free.sem, 1)
                if near_bwd.due(h, 0):
                    dve.wait_ge(near_bwd.sem, near_bwd.at(h, 0))
                if near_fwd.due(h, 0):
                    dve.wait_ge(near_fwd.sem, near_fwd.at(h, 0))
                for c in range(NC):
                    dve.tensor_tensor_scan(g[:, c, 1:LP], ones, lf[:, c * P:(c + 1) * P], 0.0, ALU.mult,
                                           ALU.add).then_inc(summed.sem, 1)

            def maxima(h, t):
                if neg_peak.due(h, t):
                    dve.wait_ge(neg_peak.sem, neg_peak.at(h, t))
                for c in range(2):
                    i = 2 * t + c
                    dve.wait_ge(S[c].full.sem, S[c].full.at(h, t + 1))
                    dve.tensor_reduce(row_max[:, i:i + 1], S[c][:], AX_X, ALU.max).then_inc(peak.sem, 1)
                dve.wait_ge(peak.sem, peak.at(h, 2 * t + 2))
                dve.tensor_scalar(neg_max[:, 2 * t:2 * t + 2], row_max[:, 2 * t:2 * t + 2], -SCALE, None,
                                  ALU.mult).then_inc(neg_peak.sem, 1)

            def mixes(h, t):
                a, b = weight[:, 2 * t:2 * t + 1], weight[:, 2 * t + 1:2 * t + 2]
                dve.wait_ge(S[0].free.sem, S[0].free.at(h, t + 1))
                dve.wait_ge(S[1].free.sem, S[1].free.at(h, t + 1))
                if mixing.due(h, 4 * t):
                    dve.wait_ge(mixing.sem, mixing.at(h, 4 * t))
                dve.reciprocal(weight[:, 2 * t:2 * t + 2], row_sum[:, 2 * t:2 * t + 2]).then_inc(mixing.sem, 1)
                dve.wait_ge(mixing.sem, mixing.at(h, 4 * t + 1))
                dve.tensor_tensor(b, b, lam_t, ALU.mult).then_inc(mixing.sem, 1)
                dve.wait_ge(mixing.sem, mixing.at(h, 4 * t + 2))
                dve.tensor_scalar(probs[:, 1], probs[:, 1], b, None, ALU.mult).then_inc(mixing.sem, 1)
                dve.wait_ge(mixing.sem, mixing.at(h, 4 * t + 3))
                dve.wait_ge(T.full.sem, T.full.at(h, 2 + t))
                dve.scalar_tensor_tensor(out=mix[:], in0=probs[:, 0], scalar=a, in1=probs[:, 1], op0=ALU.mult,
                                         op1=ALU.subtract).then_inc(mixing.sem, 1)

            def add_out(h, js):
                for j in js:
                    bank, use = (W, j // 2 + 1) if j % 2 == 0 else (O, j // 2 + 2)
                    dve.wait_ge(bank.full.sem, bank.full.at(h, use))
                    dve.wait_ge((W if j % 2 == 0 else O).free.sem, (W if j % 2 == 0 else O).free.at(h, use - 1))
                    dve.tensor_tensor(xT[:, j], xT[:, j], bank[:], ALU.add).then_inc(bank.free.sem, 1)

            def outputs(h, m):
                use, n, w, gate, count, factor = ((1, 1, w_hg, gate_h, y_hg, 1.0) if m else
                                                  (6, 2, w_sub, gate_a, y_da, 1.0 - LAM_INIT))
                dve.wait_ge(rooted.sem, rooted.at(h, n))
                if (y_da if m else y_hg).due(h, 0 if m else 3):
                    dve.wait_ge((y_da if m else y_hg).sem, (y_da if m else y_hg).at(h, 0 if m else 3))
                dve.scalar_tensor_tensor(out=yn[:], in0=O[:], scalar=w[:, 0:1], in1=rstd[:], op0=ALU.mult,
                                         op1=ALU.mult).then_inc(O.free.sem, 1)
                dve.wait_ge(O.free.sem, O.free.at(h, use))
                bank, gate_use = bank_of(5 if m else 6)
                dve.wait_ge(bank.free.sem, bank.free.at(h, gate_use - (3 if m else 0)))
                dve.scalar_tensor_tensor(out=yn[:], in0=yn[:], scalar=factor, in1=gate[:], op0=ALU.mult,
                                         op1=ALU.mult).then_inc(count.sem, 1)
                dve.wait_ge(count.sem, count.at(h, 1))
                if O.full.due(h, -1 if m else 5):
                    dve.wait_ge(O.full.sem, O.full.at(h, -1 if m else 5))
                dve.tensor_copy(y[:, m, 0], yn[:]).then_inc(count.sem, 1)
                dve.wait_ge(count.sem, count.at(h, 2))
                dve.tensor_tensor(y[:, m, 1], yn[:], y[:, m, 0].bitcast(F32), ALU.subtract).then_inc(count.sem, 1)

            def rotate(h, n):
                bank, use = bank_of(n)
                i = 0 if n == 7 else 5
                dve.wait_ge(bank.full.sem, bank.full.at(h, use))
                if roped.due(h, i):
                    dve.wait_ge(roped.sem, roped.at(h, i))
                dve.tensor_tensor(turned[:, 0], bank[:], rope[:, 0], ALU.mult).then_inc(roped.sem, 1)
                dve.stream_shuffle(turned[:, 1], bank[:], SWAP).then_inc(bank.free.sem, 1)
                dve.wait_ge(bank.free.sem, bank.free.at(h, use))
                dve.tensor_tensor(turned[:, 1], turned[:, 1], rope[:, 1], ALU.mult).then_inc(roped.sem, 1)
                dve.wait_ge(roped.sem, roped.at(h, i + 2))
                dve.tensor_tensor(turned[:, 0], turned[:, 0], turned[:, 1], ALU.add).then_inc(roped.sem, 1)
                dve.wait_ge(roped.sem, roped.at(h, i + 3))
                if (k_moved if n == 7 else q_moved).due(h, 0 if n == 7 else 4):
                    dve.wait_ge((k_moved if n == 7 else q_moved).sem, (k_moved if n == 7 else q_moved).at(h, 0 if n == 7 else 4))
                dve.tensor_copy(parts[:, 0], turned[:, 0]).then_inc(roped.sem, 1)
                dve.wait_ge(roped.sem, roped.at(h, i + 4))
                dve.tensor_tensor(parts[:, 1], turned[:, 0], parts[:, 0].bitcast(F32),
                                  ALU.subtract).then_inc(roped.sem, 1)

            def far_differences(h):
                if near_scaled.due(h, 0):
                    dve.wait_ge(near_scaled.sem, near_scaled.at(h, 0))
                edge = lambda g: g[:, 0:3, P:LP].broadcast_to([P, 3, P])
                flat = decay[:, :, :].rearrange("p a t -> p (a t)")
                dve.wait_ge(summed.sem, summed.at(h, 2 * NC))
                dve.tensor_tensor(chunked(flat[:, 0:3 * P]), edge(gf), gf[:, 0:3, 1:LP],
                                  ALU.subtract).then_inc(far_diff.sem, 1)
                dve.tensor_tensor(chunked(flat[:, 3 * P:6 * P]), edge(gb), gb[:, 0:3, 0:P],
                                  ALU.subtract).then_inc(far_diff.sem, 1)

            def both_keys(h):
                dve.wait_ge(key_exp.sem, key_exp.at(h, 2))
                if S[0].full.due(h, -5):
                    dve.wait_ge(S[0].full.sem, S[0].full.at(h, -5))
                dve.tensor_tensor(key_sum, keys[:, 0], keys[:, 1], ALU.add).then_inc(key_both.sem, 1)

            def place_diagonal(h):
                dve.wait_ge(S[0].full.sem, S[0].full.at(h, 5))
                if O.full.due(h, 1):
                    dve.wait_ge(O.full.sem, O.full.at(h, 1))
                dve.tensor_tensor(att_diag, chunked(S[0][:]), eye[:].unsqueeze(1).broadcast_to([P, NC, P]),
                                  ALU.mult).then_inc(S[0].free.sem, 1)

            def far_scale(h):
                qf, kf, qb, kb = (scaled[:, 0, 0], scaled[:, 0, 1], scaled[:, 1, 0], scaled[:, 1, 1])
                flat = decay[:, :, :].rearrange("p a t -> p (a t)")
                from_f, from_b = soft[:, 0], soft[:, 1]
                dve.wait_ge(far_exp.sem, far_exp.at(h, 5))
                dve.wait_ge(PB[0].free.sem, PB[0].free.at(h, 2))
                if S[0].full.due(h, 0):
                    dve.wait_ge(S[0].full.sem, S[0].full.at(h, 0))
                mul = lambda out, a, b: dve.tensor_tensor(out, a, b, ALU.mult).then_inc(far_scaled.sem, 1)
                by = lambda out, a, s: dve.tensor_scalar(out, a, s, None, ALU.mult).then_inc(far_scaled.sem, 1)
                mul(qf[:, 0:2 * P], query[:, P:3 * P], from_f[:, 0:2 * P])
                mul(qf[:, 3 * P:4 * P], query[:, 3 * P:4 * P], from_f[:, 2 * P:3 * P])
                mul(kf[:, 0:3 * P], keys[:, 0, 0:3 * P], flat[:, 0:3 * P])
                mul(kb[:, 0:3 * P], keys[:, 1, P:4 * P], from_b[:, 0:3 * P])
                mul(qb[:, P:3 * P], query[:, P:3 * P], flat[:, 4 * P:6 * P])
                mul(qb[:, 3 * P:4 * P], query[:, 0:P], flat[:, 3 * P:4 * P])
                dve.wait_ge(far_scaled.sem, far_scaled.at(h, 6))
                by(qf[:, 2 * P:3 * P], qf[:, 3 * P:4 * P], total[:, 0, 2:3])
                by(kf[:, 3 * P:4 * P], kf[:, 0:P], total[:, 0, 1:2])
                by(qb[:, 0:P], qb[:, 3 * P:4 * P], total[:, 1, 1:2])
                by(kb[:, 3 * P:4 * P], kb[:, 2 * P:3 * P], total[:, 1, 2:3])

            def near_differences(h, l):
                if l < 2:
                    dve.wait_ge(far_scaled.sem, far_scaled.at(h, 10))
                else:
                    dve.wait_ge(near_scaled.sem, near_scaled.at(h, 3 * (l - 1)))
                left, right = near(gf[:, :, :], l, 1)
                key_left, _ = near(buf(l)[:, 0], l)
                _, query_right = near(buf(l)[:, 1], l)
                mid = middle(gf, l)
                dve.tensor_tensor(key_left, mid, left, ALU.subtract).then_inc(near_fwd.sem, 1)
                dve.tensor_tensor(query_right, right, mid, ALU.subtract).then_inc(near_fwd.sem, 1)

            def near_scale(h, l):
                b = 1 << l
                halves = lambda ap, i: ap.rearrange("p (n h b) -> p n h b", h=2, b=b)[:, :, i, :]
                dve.wait_ge(near_exp.sem, near_exp.at(h, l + 1))
                if l < 2:
                    dve.wait_ge(S[1].full.sem, S[1].full.at(h, 6))
                else:
                    dve.wait_ge(S[l % 2].full.sem, S[l % 2].full.at(h, 6 + l // 2))
                for i in range(2):
                    dve.tensor_tensor(halves(scaled[:, l % 2, 0], i), halves(keys[:, i], i), halves(buf(l)[:, 0], i),
                                      ALU.mult).then_inc(near_scaled.sem, 1)
                dve.tensor_tensor(scaled[:, l % 2, 1], query[:], buf(l)[:, 1], ALU.mult).then_inc(near_scaled.sem, 1)

            def place_level(h, l):
                bank = S[l % 2]
                dve.wait_ge(bank.full.sem, bank.full.at(h, 7 + l // 2))
                if l == 0:
                    dve.wait_ge(S[0].free.sem, S[0].free.at(h, 5))
                else:
                    dve.wait_ge(S[(l - 1) % 2].free.sem, S[(l - 1) % 2].free.at(h, 7 + (l - 1) // 2))
                dve.sem_inc(place_go.sem, 1)
                dve.copy_predicated(att_diag, level_mask[:, l].unsqueeze(1).broadcast_to([P, NC, P]),
                                    chunked(bank[:])).then_inc(bank.free.sem, 1)

            rotate(-1, 7)
            rotate(-1, 8)

            def iteration(h, first, last):
                gates(h, 0)
                gates(h, 1)
                maxima(h, 0)
                if not first:
                    outputs(h, 1)
                mixes(h, 0)
                maxima(h, 1)
                far_differences(h)
                mixes(h, 1)
                maxima(h, 2)
                both_keys(h)
                mixes(h, 2)
                maxima(h, 3)
                if not first:
                    add_out(h, range(0, 4))
                mixes(h, 3)
                if not first:
                    add_out(h, range(4, 8))
                place_diagonal(h)
                far_scale(h)
                near_differences(h, 0)
                near_differences(h, 1)
                if not last:
                    rotate(h, 7)
                near_scale(h, 0)
                near_differences(h, 2)
                outputs(h, 0)
                near_scale(h, 1)
                near_differences(h, 3)
                place_level(h, 0)
                near_scale(h, 2)
                if not last:
                    rotate(h, 8)
                for l in range(1, LEVELS):
                    if l + 3 < LEVELS:
                        near_differences(h, l + 3)
                    place_level(h, l)
                    if l + 2 < LEVELS:
                        near_scale(h, l + 2)

            iteration(0, True, False)
            with dve.Fori(1, HEADS - 1) as h:
                iteration(h, False, False)
            iteration(HEADS - 1, False, True)
            outputs(HEADS, 1)
            add_out(HEADS, range(8))

        @block.gpsimd
        def _(pool):
            def low(h, n):
                s = (n + 2) % 3
                pool.wait_ge(w_high.sem, w_high.at(h, n))
                pool.tensor_tensor(w_lo[:, s], w_raw[:, s], w_hi[:, s].bitcast(F32),
                                   ALU.subtract).then_inc(w_low.sem, 1)

            def low_out(h, m):
                pool.wait_ge(o_high.sem, o_high.at(h, m + 1))
                pool.tensor_tensor(o_lo[:, m], o_raw[:], o_hi[:, m].bitcast(F32),
                                   ALU.subtract).then_inc(o_low.sem, 1)

            def near_differences(h, l):
                if l < 2:
                    pool.wait_ge(far_scaled.sem, far_scaled.at(h, 10))
                else:
                    pool.wait_ge(near_scaled.sem, near_scaled.at(h, 3 * (l - 1)))
                left, right = near(gb[:, :, :], l, 0)
                _, key_right = near(buf(l)[:, 0], l)
                query_left, _ = near(buf(l)[:, 1], l)
                mid = middle(gb, l)
                pool.tensor_tensor(key_right, right, mid, ALU.subtract).then_inc(near_bwd.sem, 1)
                pool.tensor_tensor(query_left, mid, left, ALU.subtract).then_inc(near_bwd.sem, 1)

            for n in (-2, -1, 0, 1, 2):
                low(0, n)

            def iteration(h, last):
                for n in range(3, 7 if last else 9):
                    low(h, n)
                low_out(h, 0)
                if not last:
                    low(h, 9)
                near_differences(h, 0)
                near_differences(h, 1)
                if not last:
                    low(h, 10)
                near_differences(h, 2)
                if not last:
                    low(h, 11)
                low_out(h, 1)
                for l in range(3, LEVELS):
                    near_differences(h, l)

            iteration(0, False)
            with pool.Fori(1, HEADS - 1) as h:
                iteration(h, False)
            iteration(HEADS - 1, True)


def odd_layer(nc, xT, eye, ones, rope, eps, w_in, w_out, norm, norm_out, sink_d, band_d, out):
    with ExitStack() as ctx:
        sb = lambda name, shape, dt=F32: ctx.enter_context(nc.sbuf_tensor(name, shape, dt))
        sem = lambda name, *a, **k: Count(ctx.enter_context(nc.semaphore(name)), *a, **k)
        SLOTS = 4

        hH, hL = sb("hH2", [P, KT, SEQ], F32R), sb("hL2", [P, KT, SEQ], F32R)
        w_raw = sb("w_raw2", [P, SLOTS, KT, P])
        w_hi, w_lo = sb("w_hi2", [P, SLOTS, KT, P], F32R), sb("w_lo2", [P, SLOTS, KT, P], F32R)
        o_raw = sb("o_raw2", [P, DM])
        o_hi, o_lo = sb("o_hi2", [P, 2, DM], F32R), sb("o_lo2", [P, 2, DM], F32R)
        y = sb("y2", [P, 2, 2, SEQ], F32R)
        parts = sb("parts2", [P, 2, SEQ], F32R)
        qs = sb("qs2", [P, 2, 2, SEQ], F32R)
        ks = sb("ks2", [P, 4 * 2 * SEQ], F32R)
        v = sb("v2", [P, NC, 4 * HD])
        probs = sb("probs2", [P, 2, 2, 3 * P])
        probsT = sb("probsT", [P, 2, 2, 3 * P])
        normed = sb("normed", [P, SEQ])
        gate = sb("gate2", [P, 2, SEQ])
        gated = sb("gated", [P, 2, SEQ])
        vt = sb("vt2", [P, SEQ])
        turned = sb("turned2", [P, 2, SEQ])
        soft = sb("soft2", [P, 2, SEQ])
        rstd = sb("rstd2", [P, SEQ])
        staged = sb("staged", [P, 2, DM])
        small = sb("small2", [P, 64])
        sink, neg_sink = sb("sink", [P, 2 * PAIRS]), sb("neg_sink", [P, 2 * PAIRS])
        wn, w_final = sb("wn2", [P, KT]), sb("w_final", [P, KT])
        band_raw = sb("band_raw", [P, 2, P])
        band, eye_b = sb("band", [P, 2, P], BF16), sb("eye_b", [P, P], BF16)
        final = w_raw[:, :, :, :].rearrange("p s k c -> p (s k c)").rearrange("p (k t) -> p k t", t=SEQ)

        row_max, neg_max = small[:, 0:16], small[:, 16:32]
        row_sum, weight = small[:, 32:48], small[:, 48:64]

        PB = [Bank(nc, ctx, f"odd_proj{b}", 2, 3) for b in range(2)]
        S = [Bank(nc, ctx, f"odd_score{a}", 8) for a in range(2)]
        T = [Bank(nc, ctx, f"odd_turn{a}", 8) for a in range(2)]
        O, W = Bank(nc, ctx, "odd_out", 2), Bank(nc, ctx, "odd_wide", 10, -9)

        ready, landed = sem("odd_constants_ready"), sem("odd_constants_landed", unit=DMA)
        w_in_sem = [sem(f"odd_weights{i}_landed", 1, 1 + i // 2, unit=DMA) for i in range(SLOTS)]
        load_go = sem("odd_load_go")
        w_high, w_low = sem("odd_weights_high", 4, 6), sem("odd_weights_low", 4, 6)
        o_in = sem("odd_out_weights_landed", 2, 0, unit=DMA)
        o_high, o_low = sem("odd_out_weights_high", 2), sem("odd_out_weights_low", 2)
        peak, neg_peak = sem("odd_row_max", 16), sem("odd_neg_row_max", 8)
        roped = sem("odd_roped", 10, 15)
        k_moved, q_moved = sem("odd_k_moved", unit=DMA), sem("odd_q_moved", 8, 4, unit=DMA)
        v_turned, v_kept = sem("odd_v_turned"), sem("odd_v_kept")
        sink_shift, sink_exp = sem("sink_shifted", 2), sem("sink_exp", 2)
        weighed = sem("weighed", 4)
        split = sem("odd_y_split", 4, -2)
        turned_out, kept = sem("out_turned"), [sem(f"out_kept{i}") for i in range(2)]
        stores = [sem(f"stored{i}", unit=DMA) for i in range(2)]
        nrm = Norm(nc, ctx, "norm_odd", xT, wn, ones, eps, turned, soft, rstd[:], O, hH, hL)
        nrm_out = Norm(nc, ctx, "norm_final", xT, w_final, ones, eps, turned, soft, rstd[:], O)

        w_cols = w_in.rearrange("(k p) n -> p k n", p=P)

        def bank_of(n):
            return PB[(n - 1) % 2], (n - 1) // 2 + 1


        def key_head(h, half):
            return 2 * half + h // 4

        def window(t):
            lo, hi = max(0, t - 1), min(NC - 1, t + 1)
            return lo, hi - lo + 1

        def tile_use(half, t):
            return NC * half + t + 1

        def turn_of(half, steady):
            return 5 * half + 1 if steady else 10

        block = ctx.enter_context(nc.Block())

        @block.sync
        def _(sp):
            sp.dma_start(sink[:], sink_d.broadcast_to([P, 2 * PAIRS])).then_inc(landed.sem, DMA)
            for to, of in ((wn, norm), (w_final, norm_out), (band_raw, band_d)):
                sp.dma_start(to[:], of).then_inc(landed.sem, DMA)

            def load(h, n):
                if w_low.due(h, n - SLOTS):
                    sp.wait_ge(w_low.sem, w_low.at(h, n - SLOTS))
                sp.sem_inc(load_go.sem, 1)
                gates = DI + 4 * P
                if n <= 0:
                    col = {-5: DI, -3: DI + P, -4: DI + 2 * P, -2: DI + 3 * P, -1: 0, 0: gates}[n]
                else:
                    col = (KT * P, gates + KT * P, P, gates + P)[(n - 1) % 4] + (h + (n - 1) // 4) * P
                s = (n + 3) % SLOTS
                sp.dma_start(w_raw[:, s], w_cols[:, :, bass.ds(col, P)]).then_inc(w_in_sem[s].sem, DMA)

            def load_out(h, m):
                if o_low.due(h, m):
                    sp.wait_ge(o_low.sem, o_low.at(h, m))
                sp.sem_inc(load_go.sem, 1)
                row = m * DM + h * P
                sp.dma_start(o_raw[:], w_out[bass.ds(row, P), :]).then_inc(o_in.sem, DMA)

            def move_q(h, half, roped_to):
                sp.wait_ge(roped.sem, roped.at(h, roped_to))
                for c in range(2):
                    for i in range(2):
                        sp.dma_start(qs[HD * i:HD * i + HD, half, c, :].bitcast(F32),
                                     parts[HD * c:HD * c + HD, i, :].bitcast(F32)).then_inc(q_moved.sem, DMA)

            def move_k(g, roped_to):
                sp.wait_ge(roped.sem, roped.at(0, roped_to))
                for c in range(2):
                    to = ks[:, (2 * g + c) * 2 * SEQ:(2 * g + c + 1) * 2 * SEQ].rearrange("p (i t) -> p i t", i=2)
                    for i in range(2):
                        sp.dma_start(to[HD * i:HD * i + HD].bitcast(F32),
                                     parts[HD * c:HD * c + HD, :, :].bitcast(F32)).then_inc(k_moved.sem, DMA)

            for n in range(-5, 1):
                load(0, n)
            load(0, 1)
            load(0, 2)
            move_k(0, -10)
            move_k(1, -5)
            move_q(0, 0, 0)

            def iteration(h, last):
                if not last:
                    load(h, 3)
                    load(h, 4)
                if S[1].full.due(h, 0):
                    sp.wait_ge(S[1].full.sem, S[1].full.at(h, 0))
                sp.sem_inc(load_go.sem, 1)
                move_q(h, 1, 5)
                load_out(h, 0)
                if not last:
                    load(h, 5)
                    load(h, 6)
                    sp.wait_ge(S[1].full.sem, S[1].full.at(h, tile_use(0, 3)))
                    sp.sem_inc(load_go.sem, 1)
                    move_q(h, 0, 10)
                load_out(h, 1)

            iteration(0, False)
            with sp.Fori(1, HEADS - 1) as h:
                iteration(h, False)
            iteration(HEADS - 1, True)

            for t in range(NC):
                sp.wait_ge(kept[0].sem, kept[0].at(0, t + 1))
                sp.wait_ge(kept[1].sem, kept[1].at(0, t + 1))
                sp.dma_start(out[t * P:(t + 1) * P, :], staged[:, t % 2]).then_inc(stores[t % 2].sem, DMA)
            sp.wait_ge(stores[0].sem, stores[0].at(0, 2))
            sp.wait_ge(stores[1].sem, stores[1].at(0, 2))

        @block.tensor
        def _(pe):
            def proj(h, n, half=None):
                bank, use = bank_of(n)
                if half != 1:
                    pe.wait_ge(w_low.sem, w_low.at(h, n))
                    if bank.free.due(h, use - 1):
                        pe.wait_ge(bank.free.sem, bank.free.at(h, use - 1))
                s = (n + 3) % SLOTS
                tiles = range(KT) if half is None else range(half * KT // 2, (half + 1) * KT // 2)
                for k in tiles:
                    mm = split_product(pe, bank[:], w_hi[:, s, k], w_lo[:, s, k], hH[:, k], hL[:, k],
                                       k == 0, k == KT - 1)
                if half != 0:
                    mm.then_inc(bank.full.sem, 1)

            def scores(h, half, t):
                lo, n = window(t)
                if t == 0:
                    pe.wait_ge(q_moved.sem, q_moved.at(h, 4 * half))
                for a in range(2):
                    if S[a].free.due(h, tile_use(half, t) - 1):
                        pe.wait_ge(S[a].free.sem, S[a].free.at(h, tile_use(half, t) - 1))
                    at, query = S[a][:, 0:n * P], qs[:, half, a, t * P:(t + 1) * P]
                    for part in range(2):
                        keys = ks[:, bass.ds((2 * key_head(h, half) + part) * SEQ + lo * P, n * P)]
                        mm = pe.matmul(at, query, keys, start=part == 0, stop=False)
                    if t > 0:
                        mm = pe.matmul(S[a][:, 0:P], eye_b[:], band[:, 0], start=False, stop=t == NC - 1)
                    if t < NC - 1:
                        mm = pe.matmul(S[a][:, (n - 1) * P:n * P], eye_b[:], band[:, 1], start=False, stop=True)
                    mm.then_inc(S[a].full.sem, 1)

            def turns(h, half, t):
                _, n = window(t)
                for a in range(2):
                    use = tile_use(half, t)
                    pe.wait_ge(S[a].free.sem, S[a].free.at(h, tile_use(half, t)))
                    if T[a].free.due(h, use - 1):
                        pe.wait_ge(T[a].free.sem, T[a].free.at(h, use - 1))
                    for j in range(n):
                        mm = pe.transpose(T[a][:, j * P:(j + 1) * P], probs[:, t % 2, a, j * P:(j + 1) * P], eye[:])
                    mm.then_inc(T[a].full.sem, 1)

            def values(h, half, t):
                lo, n = window(t)
                if t == 0:
                    if O.free.due(h, half):
                        pe.wait_ge(O.free.sem, O.free.at(h, half))
                for a in range(2):
                    pe.wait_ge(T[a].free.sem, T[a].free.at(h, tile_use(half, t)))
                    col = (2 * t + a) * HD
                    for j in range(n):
                        mm = pe.matmul(O[:, col:col + HD], probsT[:, t % 2, a, j * P:(j + 1) * P],
                                       v[:, lo + j, bass.ds(key_head(h, half) * HD, HD)], start=j == 0, stop=j == n - 1)
                if t == NC - 1:
                    mm.then_inc(O.full.sem, 1)

            def turn_out(h_before, before, use):
                if W.free.due(h_before + before, use - 1):
                    pe.wait_ge(W.free.sem, W.free.at(h_before + before, use - 1))
                pe.wait_ge(O.free.sem, O.free.at(h_before, before + 1))
                for t in range(NC):
                    mm = pe.transpose(W[:, t * P:(t + 1) * P], normed[:, t * P:(t + 1) * P], eye[:])
                mm.then_inc(W.full.sem, 1)

            def out_tiles(h, js, use):
                pe.wait_ge(split.sem, split.at(h, 2))
                pe.wait_ge(o_low.sem, o_low.at(h, 0))
                for j in js:
                    pe.wait_ge(W.free.sem, W.free.at(h, use - 1))
                    for m in range(2):
                        mm = split_product(pe, W[:], o_hi[:, m, j * P:(j + 1) * P], o_lo[:, m, j * P:(j + 1) * P],
                                           y[:, m, 0], y[:, m, 1], m == 0, m == 1)
                    mm.then_inc(W.full.sem, 1)
                    use += 1

            pe.wait_ge(ready.sem, ready.at(0, 3))
            nrm.pe(pe)
            pe.wait_ge(nrm.low.sem, nrm.low.at(0, KT))
            pe.wait_ge(nrm.logged.sem, nrm.logged.at(0, 1))

            def turn_values(g):
                pe.wait_ge(PB[1].free.sem, PB[1].free.at(0, g - 2))
                if v_kept.due(0, g):
                    pe.wait_ge(v_kept.sem, v_kept.at(0, g))
                for c in range(NC):
                    mm = pe.transpose(T[0][:, c * P:(c + 1) * P], vt[:, c * P:(c + 1) * P], eye[:])
                mm.then_inc(v_turned.sem, 1)

            for n in (-5, -4, -3):
                proj(0, n)
            turn_values(0)
            proj(0, -2)
            proj(0, -1)
            turn_values(1)
            proj(0, 0)
            pe.wait_ge(v_kept.sem, v_kept.at(0, 2))
            pe.wait_ge(k_moved.sem, k_moved.at(0, 8))

            def half_step(h, half, zeroth, last):
                n = 1 if half == 0 else 3
                before, h_before = 1 - half, (h if half else h - 1)
                first, project, outs = zeroth and not half, not (last and half), not zeroth
                scores(h, half, 0)
                if project:
                    proj(h, n, 0)
                if not first:
                    turns(h_before, before, 3)
                if project:
                    proj(h, n, 1)
                if not first:
                    values(h_before, before, 3)
                scores(h, half, 1)
                turns(h, half, 0)
                if project:
                    proj(h, n + 1, 0)
                values(h, half, 0)
                scores(h, half, 2)
                turns(h, half, 1)
                if project:
                    proj(h, n + 1, 1)
                values(h, half, 1)
                if not first:
                    turn_out(h_before, before, turn_of(half, outs))
                scores(h, half, 3)
                turns(h, half, 2)
                if outs:
                    out_tiles(h, range(4 * half, 4 * half + 2), 5 * half + 2)
                values(h, half, 2)
                if outs:
                    out_tiles(h, range(4 * half + 2, 4 * half + 4), 5 * half + 4)

            def iteration(h, zeroth, last):
                half_step(h, 0, zeroth, last)
                half_step(h, 1, zeroth, last)

            iteration(0, True, False)
            with pe.Fori(1, HEADS - 1) as h:
                iteration(h, False, False)
            iteration(HEADS - 1, False, True)
            turns(HEADS - 1, 1, 3)
            values(HEADS - 1, 1, 3)
            turn_out(HEADS - 1, 1, 1)
            out_tiles(HEADS, range(8), 2)

            nrm_out.pe(pe)
            for t in range(NC):
                for i in range(2):
                    if kept[i].due(0, t):
                        pe.wait_ge(kept[i].sem, kept[i].at(0, t))
                    for k in range(4):
                        pe.wait_ge(nrm_out.scaled_to.sem, nrm_out.scaled_to.at(0, 4 * i + k + 1))
                        mm = pe.transpose(S[i][:, k * P:(k + 1) * P], final[:, 4 * i + k, t * P:(t + 1) * P], eye[:])
                    mm.then_inc(turned_out.sem, 1)

        @block.scalar
        def _(act):
            def high(h, n):
                s = (n + 3) % SLOTS
                act.wait_ge(w_in_sem[s].sem, w_in_sem[s].at(h, (n + 3) // SLOTS))
                bank, use = bank_of(n - SLOTS)
                if bank.full.due(h, use):
                    act.wait_ge(bank.full.sem, bank.full.at(h, use))
                act.activation(w_hi[:, s], w_raw[:, s], ACT.Copy).then_inc(w_high.sem, 1)

            def high_out(h, m):
                act.wait_ge(o_in.sem, o_in.at(h, m + 1))
                act.wait_ge(W.full.sem, W.full.at(h, 10))
                act.activation(o_hi[:, m], o_raw[:], ACT.Copy).then_inc(o_high.sem, 1)

            def soft_max(h, half, t):
                _, n = window(t)
                act.wait_ge(neg_peak.sem, neg_peak.at(h, tile_use(half, t)))
                for a in range(2):
                    i = 8 * half + 2 * t + a
                    if T[a].full.due(h, tile_use(half, t) - 2):
                        act.wait_ge(T[a].full.sem, T[a].full.at(h, tile_use(half, t) - 2))
                    act.activation(probs[:, t % 2, a, 0:n * P], S[a][:, 0:n * P], ACT.Exp, bias=neg_max[:, i:i + 1],
                                   scale=SCALE, accum_out=row_sum[:, i:i + 1]).then_inc(S[a].free.sem, 1)

            def keep_turn(h, half, t):
                _, n = window(t)
                act.wait_ge(T[0].full.sem, T[0].full.at(h, tile_use(half, t)))
                act.activation(probsT[:, t % 2, 0, 0:n * P], T[0][:, 0:n * P], ACT.Copy).then_inc(T[0].free.sem, 1)

            def exp_sink(h, half):
                act.wait_ge(sink_shift.sem, sink_shift.at(h, half + 1))
                at = weight[:, 8 * half:8 * half + 8]
                act.activation(at, at, ACT.Exp).then_inc(sink_exp.sem, 1)

            def silu(h, n, half, zeroth=False):
                bank, use = bank_of(n)
                act.wait_ge(bank.full.sem, bank.full.at(h, use))
                if not zeroth:
                    if W.free.due(h, turn_of(n // 4, True)):
                        act.wait_ge(W.free.sem, W.free.at(h, turn_of(n // 4, True)))
                act.activation(gate[:, half], bank[:], ACT.Silu).then_inc(bank.free.sem, 1)

            nrm.act(act)
            for n in range(-5, 0):
                high(0, n)

            def take_values(g):
                act.wait_ge(PB[1].full.sem, PB[1].full.at(0, g - 2))
                if v_turned.due(0, g):
                    act.wait_ge(v_turned.sem, v_turned.at(0, g))
                act.activation(vt[:], PB[1][:], ACT.Copy).then_inc(PB[1].free.sem, 1)

            def keep_values(g):
                act.wait_ge(v_turned.sem, v_turned.at(0, g + 1))
                act.activation(v[:, :, g * P:(g + 1) * P], chunked(T[0][:]), ACT.Copy).then_inc(v_kept.sem, 1)

            take_values(0)
            high(0, 0)
            high(0, 1)
            keep_values(0)
            take_values(1)
            high(0, 2)
            keep_values(1)
            silu(0, 0, 0, True)

            def half_step(h, half, zeroth, last):
                before, h_before = 1 - half, (h if half else h - 1)
                n = 3 + 2 * half
                soft_max(h, half, 0)
                if not (zeroth and not half):
                    keep_turn(h_before, before, 3)
                if not last:
                    high(h, n)
                soft_max(h, half, 1)
                keep_turn(h, half, 0)
                soft_max(h, half, 2)
                if not last:
                    high(h, n + 1)
                keep_turn(h, half, 1)
                soft_max(h, half, 3)
                exp_sink(h, half)
                keep_turn(h, half, 2)
                if not (last and half):
                    silu(h, 2 + 2 * half, 1 - half, zeroth and not half)

            def iteration(h, zeroth, last):
                half_step(h, 0, zeroth, last)
                half_step(h, 1, zeroth, last)
                high_out(h, 0)
                high_out(h, 1)

            iteration(0, True, False)
            with act.Fori(1, HEADS - 1) as h:
                iteration(h, False, False)
            iteration(HEADS - 1, False, True)
            keep_turn(HEADS - 1, 1, 3)
            act.wait_ge(W.free.sem, W.free.at(HEADS, 9))
            nrm_out.act(act)
            for t in range(NC):
                act.wait_ge(turned_out.sem, turned_out.at(0, 2 * t + 1))
                if t >= 2:
                    act.wait_ge(stores[t % 2].sem, stores[t % 2].at(0, 1))
                act.activation(staged[:, t % 2, 0:SEQ], S[0][:], ACT.Copy).then_inc(kept[0].sem, 1)

        @block.vector
        def _(dve):
            dve.wait_ge(landed.sem, landed.at(0, 4))
            dve.tensor_scalar(neg_sink[:], sink[:], -1.0, None, ALU.mult).then_inc(ready.sem, 1)
            dve.tensor_copy(band[:], band_raw[:]).then_inc(ready.sem, 1)
            dve.tensor_copy(eye_b[:], eye[:]).then_inc(ready.sem, 1)
            dve.wait_ge(ready.sem, ready.at(0, 3))
            nrm.dve(dve)

            def rotate(h, n):
                bank, use = bank_of(n)
                i = {-5: -15, -3: -10, -1: -5, 1: 0, 3: 5}[n]
                dve.wait_ge(bank.full.sem, bank.full.at(h, use))
                if roped.due(h, i):
                    dve.wait_ge(roped.sem, roped.at(h, i))
                dve.tensor_tensor(turned[:, 0], bank[:], rope[:, 0], ALU.mult).then_inc(roped.sem, 1)
                dve.stream_shuffle(turned[:, 1], bank[:], SWAP).then_inc(bank.free.sem, 1)
                dve.wait_ge(bank.free.sem, bank.free.at(h, use))
                dve.tensor_tensor(turned[:, 1], turned[:, 1], rope[:, 1], ALU.mult).then_inc(roped.sem, 1)
                dve.wait_ge(roped.sem, roped.at(h, i + 2))
                dve.tensor_tensor(turned[:, 0], turned[:, 0], turned[:, 1], ALU.add).then_inc(roped.sem, 1)
                dve.wait_ge(roped.sem, roped.at(h, i + 3))
                if n in (-3, -1):
                    dve.wait_ge(k_moved.sem, k_moved.at(0, 2 * n + 10))
                elif n > 0:
                    dve.wait_ge(q_moved.sem, q_moved.at(h, 4 * (n // 2)))
                dve.tensor_copy(parts[:, 0], turned[:, 0]).then_inc(roped.sem, 1)
                dve.wait_ge(roped.sem, roped.at(h, i + 4))
                dve.tensor_tensor(parts[:, 1], turned[:, 0], parts[:, 0].bitcast(F32),
                                  ALU.subtract).then_inc(roped.sem, 1)

            def maxima(h, half, t):
                _, n = window(t)
                i = 8 * half + 2 * t
                for a in range(2):
                    dve.wait_ge(S[a].full.sem, S[a].full.at(h, tile_use(half, t)))
                    dve.tensor_reduce(row_max[:, i + a:i + a + 1], S[a][:, 0:n * P], AX_X,
                                      ALU.max).then_inc(peak.sem, 1)
                dve.wait_ge(peak.sem, peak.at(h, i + 2))
                sinks = neg_sink[:, bass.ds(2 * KT * half + 2 * h, 2)]
                dve.scalar_tensor_tensor(out=neg_max[:, i:i + 2], in0=row_max[:, i:i + 2], scalar=-SCALE, in1=sinks,
                                         op0=ALU.mult, op1=ALU.min).then_inc(neg_peak.sem, 1)

            def keep_turn(h, half, t):
                _, n = window(t)
                dve.wait_ge(T[1].full.sem, T[1].full.at(h, tile_use(half, t)))
                dve.tensor_copy(probsT[:, t % 2, 1, 0:n * P], T[1][:, 0:n * P]).then_inc(T[1].free.sem, 1)

            def shift_sink(h, half):
                dve.wait_ge(neg_peak.sem, neg_peak.at(h, tile_use(half, NC - 1)))
                sinks = sink[:, bass.ds(2 * KT * half + 2 * h, 2)].unsqueeze(1).broadcast_to([P, NC, 2])
                by_tile = lambda ap: ap[:, 8 * half:8 * half + 8].rearrange("p (t a) -> p t a", a=2)
                dve.tensor_tensor(by_tile(weight), by_tile(neg_max), sinks, ALU.add).then_inc(sink_shift.sem, 1)

            def weigh(h, half):
                at = slice(8 * half, 8 * half + 8)
                dve.wait_ge(sink_exp.sem, sink_exp.at(h, half + 1))
                for a in range(2):
                    dve.wait_ge(S[a].free.sem, S[a].free.at(h, tile_use(half, NC - 1)))
                dve.tensor_tensor(weight[:, at], weight[:, at], row_sum[:, at], ALU.add).then_inc(weighed.sem, 1)
                dve.wait_ge(weighed.sem, weighed.at(h, 2 * half + 1))
                dve.reciprocal(weight[:, at], weight[:, at]).then_inc(weighed.sem, 1)

            def normalize(h, half):
                dve.wait_ge(weighed.sem, weighed.at(h, 2 * half + 2))
                dve.wait_ge(O.full.sem, O.full.at(h, half + 1))
                if O.free.due(h, half):
                    dve.wait_ge(O.free.sem, O.free.at(h, half))
                by_head = lambda ap: ap.rearrange("p (g f) -> p g f", f=HD)
                scale = weight[:, 8 * half:8 * half + 8].unsqueeze(2).broadcast_to([P, 8, HD])
                dve.tensor_tensor(by_head(normed[:]), by_head(O[:]), scale, ALU.mult).then_inc(O.free.sem, 1)

            def apply_gate(h, before, use):
                dve.wait_ge(W.full.sem, W.full.at(h, use))
                dve.tensor_tensor(gated[:, before], W[:], gate[:, before], ALU.mult).then_inc(W.free.sem, 1)

            def split_y(h, half, use):
                i = 0 if half else 2
                dve.wait_ge(W.free.sem, W.free.at(h, use))
                dve.wait_ge(W.full.sem, W.full.at(h, 0 if half else 10))
                dve.tensor_copy(y[:, half, 0], gated[:, half]).then_inc(split.sem, 1)
                dve.wait_ge(split.sem, split.at(h, i + 1))
                dve.tensor_tensor(y[:, half, 1], gated[:, half], y[:, half, 0].bitcast(F32),
                                  ALU.subtract).then_inc(split.sem, 1)

            def add_out(h, js, use):
                for j in js:
                    dve.wait_ge(W.full.sem, W.full.at(h, use))
                    dve.wait_ge(W.free.sem, W.free.at(h, use - 1))
                    dve.tensor_tensor(xT[:, j], xT[:, j], W[:], ALU.add).then_inc(W.free.sem, 1)
                    use += 1

            rotate(0, -5)
            rotate(0, -3)
            rotate(0, -1)

            def half_step(h, half, zeroth, last):
                before, h_before = 1 - half, (h if half else h - 1)
                first, use = zeroth and not half, turn_of(half, not zeroth)
                maxima(h, half, 0)
                if not first:
                    keep_turn(h_before, before, 3)
                    weigh(h_before, before)
                    normalize(h_before, before)
                maxima(h, half, 1)
                keep_turn(h, half, 0)
                if not (last and half):
                    rotate(h, 2 * half + 1)
                maxima(h, half, 2)
                keep_turn(h, half, 1)
                if not first:
                    apply_gate(h, before, use)
                if not half and not first:
                    split_y(h, 1, use)
                maxima(h, half, 3)
                shift_sink(h, half)
                keep_turn(h, half, 2)
                if not zeroth:
                    add_out(h, range(4 * half, 4 * half + 4), 5 * half + 2)
                if half:
                    split_y(h, 0, use)

            def iteration(h, zeroth, last):
                half_step(h, 0, zeroth, last)
                half_step(h, 1, zeroth, last)

            iteration(0, True, False)
            with dve.Fori(1, HEADS - 1) as h:
                iteration(h, False, False)
            iteration(HEADS - 1, False, True)
            keep_turn(HEADS - 1, 1, 3)
            weigh(HEADS - 1, 1)
            normalize(HEADS - 1, 1)
            apply_gate(HEADS, 1, 1)
            split_y(HEADS, 1, 1)
            add_out(HEADS, range(8), 2)
            dve.wait_ge(W.free.sem, W.free.at(HEADS, 9))
            nrm_out.dve(dve, final)
            for t in range(NC):
                dve.wait_ge(turned_out.sem, turned_out.at(0, 2 * t + 2))
                if t >= 2:
                    dve.wait_ge(stores[t % 2].sem, stores[t % 2].at(0, 1))
                dve.tensor_copy(staged[:, t % 2, SEQ:DM], S[1][:]).then_inc(kept[1].sem, 1)

        @block.gpsimd
        def _(pool):
            def low(h, n):
                s = (n + 3) % SLOTS
                pool.wait_ge(w_high.sem, w_high.at(h, n))
                pool.tensor_tensor(w_lo[:, s], w_raw[:, s], w_hi[:, s].bitcast(F32),
                                   ALU.subtract).then_inc(w_low.sem, 1)

            def low_out(h, m):
                pool.wait_ge(o_high.sem, o_high.at(h, m + 1))
                pool.tensor_tensor(o_lo[:, m], o_raw[:], o_hi[:, m].bitcast(F32),
                                   ALU.subtract).then_inc(o_low.sem, 1)

            for n in range(-5, 3):
                low(0, n)

            def iteration(h, last):
                if not last:
                    for n in range(3, 7):
                        low(h, n)
                low_out(h, 0)
                low_out(h, 1)

            iteration(0, False)
            with pool.Fori(1, HEADS - 1) as h:
                iteration(h, False)
            iteration(HEADS - 1, True)


def hybrid_encoder(nc, x, norm_even, w_in_even, lambda_qk, subln_w, hgrn_norm_w, w_out_even, norm_odd, w_in_odd,
                   sink_logits, w_out_odd, final_norm, rope_d, levels_d, eye_d, band_d, out):
    with ExitStack() as ctx:
        sb = lambda name, shape, dt=F32: ctx.enter_context(nc.sbuf_tensor(name, shape, dt))
        xT = sb("xT", [P, KT, SEQ])
        eye, ones, eps = sb("eye", [P, P]), sb("ones", [P, P]), sb("eps", [P, 1])
        rope = sb("rope", [P, 2, SEQ])
        even_layer(nc, xT, eye, ones[:], rope, eps[:], x, w_in_even, w_out_even, norm_even, lambda_qk, subln_w,
                   hgrn_norm_w, rope_d, levels_d, eye_d)
        odd_layer(nc, xT, eye, ones[:], rope, eps[:], w_in_odd, w_out_odd, norm_odd, final_norm, sink_logits,
                  band_d, out)


def constants():
    f32 = np.float32
    inv = f32(500000.0) ** (-np.arange(0, ROPE, 2, dtype=f32) / f32(ROPE))
    ang = np.arange(SEQ, dtype=f32)[None, :] * inv[:, None].astype(f32)
    cos, sin = np.cos(ang).astype(f32), np.sin(ang).astype(f32)
    rope = np.zeros((P, 2, SEQ), f32)
    rope[:, 0] = 1.0
    n = ROPE // 2
    for base in (0, HD):
        rope[base:base + n, 0] = rope[base + n:base + 2 * n, 0] = cos
        rope[base:base + n, 1] = -sin
        rope[base + n:base + 2 * n, 1] = sin
    i = np.arange(P)
    levels = np.stack([(i[:, None] >> l + 1 == i[None, :] >> l + 1) & (i[:, None] >> l != i[None, :] >> l)
                       for l in range(LEVELS)], 1).astype(f32)
    q, k = i[:, None], i[None, :]
    band = np.stack([np.where(k >= q, 0.0, MASKED), np.where(k <= q, 0.0, MASKED)], 1).astype(f32)
    return {"rope": rope, "levels": levels, "eye": np.eye(P, dtype=f32), "band": band}


def kernel(x, norm_even, w_in_even, lambda_qk, subln_w, hgrn_norm_w, hgrn_lb_logits, w_out_even, norm_odd, w_in_odd,
           sink_logits, w_out_odd, final_norm):
    import concourse.bacc as bacc
    from concourse.bass_utils import run_bass_kernel_spmd as run

    x, w_in_even, w_out_even = np.asarray(x), np.asarray(w_in_even), np.asarray(w_out_even)
    assert x.shape == (1, SEQ, DM) and np.asarray(hgrn_lb_logits).shape[1] == 1
    column = lambda a, n: np.ascontiguousarray(np.asarray(a).reshape(n, P).T)
    const = constants()
    arrays = {
        "x": x[0], "norm_even": column(norm_even, KT), "w_in_even": w_in_even[0],
        "lambda_qk": np.asarray(lambda_qk).reshape(1, 4 * HD), "subln_w": column(subln_w, 1),
        "hgrn_norm_w": column(hgrn_norm_w, 1), "w_out_even": w_out_even[0], "norm_odd": column(norm_odd, KT),
        "w_in_odd": np.asarray(w_in_odd)[0], "sink_logits": np.asarray(sink_logits).reshape(1, 2 * PAIRS),
        "w_out_odd": np.asarray(w_out_odd)[0], "final_norm": column(final_norm, KT),
        "rope": const["rope"], "levels": const["levels"], "eye": const["eye"], "band": const["band"],
    }
    nc = bacc.Bacc("TRN2", target_bir_lowering=False, num_devices=1)
    feeds, args = {}, []
    for name, a in arrays.items():
        feeds[f"in_{name}"] = a = np.ascontiguousarray(a)
        args.append(nc.dram_tensor(f"in_{name}", a.shape, mybir.dt.from_np(a.dtype), kind="ExternalInput").ap())
    args.append(nc.dram_tensor("out", (SEQ, DM), F32, kind="ExternalOutput").ap())
    hybrid_encoder(nc, *args)
    return run(nc, [feeds], core_ids=[0]).results[0]["out"].reshape(1, SEQ, DM)
```

```python
from contextlib import ExitStack

import numpy as np

import concourse.bass as bass
from concourse import mybir

ALU = mybir.AluOpType
ACT = mybir.ActivationFunctionType
AX_X = mybir.AxisListType.X
F32 = mybir.dt.float32
F32R = mybir.dt.float32r
BF16 = mybir.dt.bfloat16
U8 = mybir.dt.uint8

P = 128
SEQ = 512
DM = 1024
KT = DM // P
DI = 2 * DM
HD = 64
ROPE = HD // 4
NC = SEQ // P
HEADS = 8
PAIRS = 16
LEVELS = 7
LP = P + 1
SCALE = HD ** -0.5
LAM_INIT = 0.8 - 0.6 * 1.0
EPS = 1e-6
MASKED = -1e30
EXP_LOG = "natural_log_exp_and_others"
DMA = 16
SWAP = list(range(ROPE // 2, ROPE)) + list(range(ROPE // 2)) + list(range(ROPE, 32))


class Count:

    def __init__(self, sem, per=0, lead=0, unit=1):
        self.sem, self.per, self.lead, self.unit = sem, per, lead, unit

    def at(self, h, n):
        return self.unit * (self.lead + self.per * h + n)

    def due(self, h, n):
        return not isinstance(self.at(h, n), int) or self.at(h, n) > 0


def chunked(ap, width=P):
    return ap.rearrange("p (c w) -> p c w", w=width)


class Bank:

    def __init__(self, nc, ctx, name, per=0, lead=0):
        self.t = ctx.enter_context(nc.psum_tensor(f"bank_{name}", [P, SEQ], F32))
        self.full = Count(ctx.enter_context(nc.semaphore(f"{name}_full")), per, lead)
        self.free = Count(ctx.enter_context(nc.semaphore(f"{name}_free")), per, lead)

    def __getitem__(self, at):
        return self.t[at]


def split_product(pe, out, hi, lo, moving_hi, moving_lo, start, stop):
    pe.matmul(out, hi, moving_hi, start=start, stop=False)
    pe.matmul(out, hi, moving_lo, start=False, stop=False)
    return pe.matmul(out, lo, moving_hi, start=False, stop=stop)


class Norm:

    def __init__(self, nc, ctx, name, xT, w, ones, eps, squares, scaled, rstd, bank, hH, hL):
        sem = lambda s: Count(ctx.enter_context(nc.semaphore(f"{name}_{s}")))
        self.squared, self.added, self.summed, self.logged = map(sem, ("squared", "added", "summed", "logged"))
        self.rooted, self.scaled_to, self.high, self.low = map(sem, ("rooted", "scaled", "high", "low"))
        self.xT, self.w, self.ones, self.eps, self.squares, self.scaled = xT, w, ones, eps, squares, scaled
        self.rstd, self.bank, self.hH, self.hL = rstd, bank, hH, hL

    def square(self, act, k):
        if k >= 4:
            act.wait_ge(self.added.sem, self.added.at(0, max(1, k - 4)))
        act.activation(self.squares[k % 4], self.xT[:, k], ACT.Square).then_inc(self.squared.sem, 1)

    def add(self, dve):
        dve.wait_ge(self.squared.sem, self.squared.at(0, 2))
        dve.tensor_tensor(self.rstd, self.squares[0], self.squares[1], ALU.add).then_inc(self.added.sem, 1)
        for k in range(2, KT):
            dve.wait_ge(self.squared.sem, self.squared.at(0, k + 1))
            dve.wait_ge(self.added.sem, self.added.at(0, k - 1))
            dve.tensor_tensor(self.rstd, self.rstd, self.squares[k % 4], ALU.add).then_inc(self.added.sem, 1)

    def sum(self, pe):
        pe.wait_ge(self.added.sem, self.added.at(0, KT - 1))
        pe.matmul(self.bank[:], self.ones, self.rstd, start=True, stop=True).then_inc(self.summed.sem, 1)

    def root(self, act):
        act.wait_ge(self.summed.sem, self.summed.at(0, 1))
        act.activation(self.rstd, self.bank[:], ACT.Ln, bias=self.eps, scale=1.0 / DM).then_inc(self.logged.sem, 1)
        act.wait_ge(self.logged.sem, self.logged.at(0, 1))
        act.activation(self.rstd, self.rstd, ACT.Exp, scale=-0.5).then_inc(self.rooted.sem, 1)

    def highs(self, act):
        for k in range(KT):
            act.wait_ge(self.scaled_to.sem, self.scaled_to.at(0, k + 1))
            act.activation(self.hH[:, k], self.scaled[:, k % 2], ACT.Copy).then_inc(self.high.sem, 1)

    def scale(self, dve):
        dve.wait_ge(self.rooted.sem, self.rooted.at(0, 1))
        for k in range(KT + 1):
            if k < KT:
                if k >= 2:
                    dve.wait_ge(self.high.sem, self.high.at(0, k - 1))
                    dve.wait_ge(self.low.sem, self.low.at(0, k - 1))
                dve.scalar_tensor_tensor(out=self.scaled[:, k % 2], in0=self.xT[:, k], scalar=self.w[:, k:k + 1],
                                         in1=self.rstd, op0=ALU.mult, op1=ALU.mult).then_inc(self.scaled_to.sem, 1)
            if k >= 1:
                dve.wait_ge(self.high.sem, self.high.at(0, k))
                dve.tensor_tensor(self.hL[:, k - 1], self.scaled[:, (k - 1) % 2], self.hH[:, k - 1].bitcast(F32),
                                  ALU.subtract).then_inc(self.low.sem, 1)

    def project(self, pe, parts, banks):
        for k in range(KT):
            pe.wait_ge(self.low.sem, self.low.at(0, k + 1))
            for (w_hi, w_lo), bank in zip(parts, banks):
                mm = split_product(pe, bank[:], w_hi[:, k], w_lo[:, k], self.hH[:, k], self.hL[:, k],
                                   k == 0, k == KT - 1)
                if k == KT - 1:
                    mm.then_inc(bank.full.sem, 1)


def even_layer(nc, xT, eye, ones, rope, eps, x, w_in, w_out, norm, lam, subln, hgw, rope_d, levels_d, eye_d):
    with ExitStack() as ctx:
        sb = lambda name, shape, dt=F32: ctx.enter_context(nc.sbuf_tensor(name, shape, dt))
        sem = lambda name, *a, **k: Count(ctx.enter_context(nc.semaphore(name)), *a, **k)

        hH, hL = sb("hH", [P, KT, SEQ], F32R), sb("hL", [P, KT, SEQ], F32R)
        w_raw = sb("w_raw", [P, 3, KT, P])
        w_hi, w_lo = sb("w_hi", [P, 3, KT, P], F32R), sb("w_lo", [P, 3, KT, P], F32R)
        o_raw = sb("o_raw", [P, DM])
        o_hi, o_lo = sb("o_hi", [P, 2, DM], F32R), sb("o_lo", [P, 2, DM], F32R)
        y = sb("y", [P, 2, 2, SEQ], F32R)
        parts = sb("parts", [P, 2, SEQ], F32R)
        qs = sb("qs", [P, 2, SEQ], F32R)
        ks = sb("ks", [P, 2, 2, SEQ], F32R)
        v = sb("v", [P, NC, P])
        probs = sb("probs", [P, 2, SEQ])
        mix = sb("mix", [P, SEQ])
        mixT = sb("mixT", [P, NC, SEQ])
        gate_a = sb("gate_a", [P, SEQ])
        vt = sb("vt", [P, SEQ])
        turned = sb("turned", [P, 2, SEQ])
        small = sb("small", [P, 64])
        gf, gb = sb("gf", [P, NC, LP]), sb("gb", [P, NC, LP])
        lf = sb("lf", [P, SEQ])
        keys = sb("keys", [P, 2, SEQ])
        query = sb("query", [P, SEQ])
        gate_h = sb("gate_h", [P, SEQ])
        vh = sb("vh", [P, NC, P])
        soft = sb("soft", [P, 2, SEQ])
        decay = sb("decay", [P, 2, SEQ])
        scaled = sb("scaled", [P, 2, 2, SEQ])
        attT = sb("attT", [P, 2560])
        sq, rstd, yn = sb("sq", [P, SEQ]), sb("rstd", [P, SEQ]), sb("yn", [P, SEQ])
        level_mask = sb("level_mask", [P, LEVELS, P], U8)
        wn = sb("wn", [P, KT])
        w_sub, w_hg = sb("w_sub", [P, 1]), sb("w_hg", [P, 1])

        row_max, neg_max = small[:, 0:8], small[:, 8:16]
        row_sum, weight = small[:, 16:24], small[:, 24:32]
        lam_t, lam_e = small[:, 32:33], small[:, 34:36]
        total = small[:, 40:48].rearrange("p (d c) -> p d c", d=2)
        att = attT[:, 0:NC * SEQ].rearrange("p (s t) -> p s t", s=NC)
        att_diag = attT[:, :].rearrange("p (c w) -> p c w", w=SEQ + P)[:, :, 0:P]
        key_sum = attT[:, NC * SEQ:2560]
        mask_raw = scaled[:, :, :, :].rearrange("p a b t -> p (a b t)")[:, 0:LEVELS * P].rearrange(
            "p (l t) -> p l t", t=P)

        PB = [Bank(nc, ctx, f"proj{b}", 3, 1) for b in range(3)]
        S = [Bank(nc, ctx, "score0", 10, 0), Bank(nc, ctx, "score1", 9, 0)]
        O, W = Bank(nc, ctx, "out", 6, -4), Bank(nc, ctx, "wide", 4, -3)
        T = Bank(nc, ctx, "turn", 8, 0)

        x_landed, landed = sem("x_landed", unit=DMA), sem("constants_landed", unit=DMA)
        x_turned, x_kept = sem("x_turned"), sem("x_kept")
        ready = sem("constants_ready")
        lam_steps = sem("lambda_steps")
        w_in_sem = [sem(f"weights{i}_landed", 3, 1, unit=DMA) for i in range(3)]
        w_high, w_low = sem("weights_high", 9, 3), sem("weights_low", 9, 3)
        o_in = sem("out_weights_landed", 2, 0, unit=DMA)
        o_high, o_low = sem("out_weights_high", 2), sem("out_weights_low", 2)
        softplus = sem("softplus", 6)
        log_f = sem("log_forget", 2)
        summed = sem("decays_summed", 2 * NC)
        key_exp = sem("keys_ready", 2)
        peak, neg_peak = sem("row_max", 8), sem("neg_row_max", 4)
        mixing = sem("mixing", 16)
        roped = sem("roped", 10, 5 * 2)
        q_moved, k_moved = sem("q_moved", 4, 4, unit=DMA), sem("k_moved", 4, 4, unit=DMA)
        squared = sem("squared", 2, -1)
        rooted = sem("rooted", 2, -1)
        y_hg, y_da = sem("y_recurrence", 3, -3), sem("y_attention", 3)
        key_both = sem("key_sum", 1)
        far_diff, far_exp = sem("far_differences", 2), sem("far_decays", 5)
        far_scaled = sem("far_scaled", 10)
        far_kept = sem("far_kept", 3)
        near_fwd, near_bwd = sem("near_differences_fwd", 2 * LEVELS), sem("near_differences_bwd", 2 * LEVELS)
        place_go = sem("place_go")
        load_go = sem("load_go")
        near_exp, near_scaled = sem("near_decays", LEVELS), sem("near_scaled", 3 * LEVELS)
        nrm = Norm(nc, ctx, "norm_even", xT, wn, ones, eps, (turned[:, 0], turned[:, 1], decay[:, 0], decay[:, 1]),
                   soft, rstd[:], O, hH, hL)

        w_cols = w_in.rearrange("(k p) n -> p k n", p=P)
        SECTION = {1: 5, 2: 6, 3: 7, 4: 4, 5: 8, 6: 3, 7: 0, 8: 1, 9: 2}

        def bank_of(n):
            return PB[(n - 1) % 3], (n - 1) // 3 + 1

        def near(ap, l, first=0):
            b = 1 << l
            if len(ap.shape) == 3:
                g = ap[:, :, first:first + P].rearrange("p c (n h b) -> p c n h b", h=2, b=b)
                return g[:, :, :, 0, :], g[:, :, :, 1, :]
            g = ap.rearrange("p (c n h b) -> p c n h b", c=NC, h=2, b=b)
            return g[:, :, :, 0, :], g[:, :, :, 1, :]

        def middle(ap, l):
            b = 1 << l
            g = ap[:, :, 0:P].rearrange("p c (n w) -> p c n w", w=2 * b)[:, :, :, b:b + 1]
            return g.broadcast_to([P, NC, P // (2 * b), b])

        def buf(l):
            return decay if l % 2 == 0 else soft

        block = ctx.enter_context(nc.Block())

        @block.sync
        def _(sp):
            tiles = (mixT[:, :, :].rearrange("p c t -> p (c t)"), attT[:, 0:2 * DM])
            for t in range(NC):
                sp.dma_start(tiles[t // 2][:, (t % 2) * DM:(t % 2 + 1) * DM],
                             x[t * P:(t + 1) * P, :]).then_inc(x_landed.sem, DMA)
            sp.dma_start(eye[:], eye_d).then_inc(x_landed.sem, DMA)
            for to, of in ((wn[:], norm), (w_sub[:], subln), (w_hg[:], hgw), (rope[:], rope_d), (mask_raw, levels_d)):
                sp.dma_start(to, of).then_inc(landed.sem, DMA)
            sp.dma_start(yn[:, 0:4 * HD], lam.broadcast_to([P, 4 * HD])).then_inc(landed.sem, DMA)

            def load(h, n):
                if w_low.due(h, n - 3):
                    sp.wait_ge(w_low.sem, w_low.at(h, n - 3))
                sp.sem_inc(load_go.sem, 1)
                head = h + 1 if n > 6 else h
                col = SECTION[(n - 1) % 9 + 1] * DM + head * P
                s = (n + 2) % 3
                sp.dma_start(w_raw[:, s], w_cols[:, :, bass.ds(col, P)]).then_inc(w_in_sem[s].sem, DMA)

            def load_out(h, m):
                if o_low.due(h, m):
                    sp.wait_ge(o_low.sem, o_low.at(h, m))
                sp.sem_inc(load_go.sem, 1)
                row = m * DM + h * P
                sp.dma_start(o_raw[:], w_out[bass.ds(row, P), :]).then_inc(o_in.sem, DMA)

            def move_q(h):
                sp.wait_ge(roped.sem, roped.at(h, 5))
                if S[1].full.due(h, 4):
                    sp.wait_ge(S[1].full.sem, S[1].full.at(h, 4))
                for c in range(2):
                    for part in range(2):
                        sp.dma_start(qs[HD * part:HD * part + HD, c, :].bitcast(F32),
                                     parts[HD * c:HD * c + HD, part, :].bitcast(F32)).then_inc(q_moved.sem, DMA)

            def move_k(h):
                sp.wait_ge(roped.sem, roped.at(h, 10))
                for c in range(2):
                    for twice in range(2):
                        sp.dma_start(ks[HD * twice:HD * twice + HD, c, :, :].bitcast(F32),
                                     parts[HD * c:HD * c + HD, :, :].bitcast(F32)).then_inc(k_moved.sem, DMA)

            for n in (-2, -1, 0):
                load(0, n)
            for n in (1, 2, 3):
                load(0, n)
            move_q(-1)
            move_k(-1)

            def iteration(h, last):
                for n in range(4, 7):
                    load(h, n)
                load_out(h, 0)
                if not last:
                    for n in range(7, 12):
                        load(h, n)
                load_out(h, 1)
                if not last:
                    load(h, 12)
                    move_q(h)
                    move_k(h)

            iteration(0, False)
            with sp.Fori(1, HEADS - 1) as h:
                iteration(h, False)
            iteration(HEADS - 1, True)

        @block.tensor
        def _(pe):
            pe.sem_inc(O.full.sem, 1)
            pe.sem_inc(W.full.sem, 1)
            pe.wait_ge(x_landed.sem, x_landed.at(0, 5))
            tiles = (mixT[:, :, :].rearrange("p c t -> p (c t)"), attT[:, 0:2 * DM])
            for k in range(KT):
                if x_kept.due(0, k - 1):
                    pe.wait_ge(x_kept.sem, x_kept.at(0, k - 1))
                for t in range(NC):
                    mm = pe.transpose(S[k % 2][:, t * P:(t + 1) * P],
                                      tiles[t // 2][:, (t % 2) * DM + k * P:(t % 2) * DM + (k + 1) * P], eye[:])
                mm.then_inc(x_turned.sem, 1)
            pe.wait_ge(ready.sem, ready.at(0, 4))
            nrm.sum(pe)

            def proj(h, n):
                bank, use = bank_of(n)
                pe.wait_ge(w_low.sem, w_low.at(h, n))
                if bank.free.due(h, use - 1):
                    pe.wait_ge(bank.free.sem, bank.free.at(h, use - 1))
                s = (n + 2) % 3
                for k in range(KT):
                    mm = split_product(pe, bank[:], w_hi[:, s, k], w_lo[:, s, k], hH[:, k], hL[:, k],
                                       k == 0, k == KT - 1)
                mm.then_inc(bank.full.sem, 1)

            def turn(h, use, of):
                if T.free.due(h, use - 1):
                    pe.wait_ge(T.free.sem, T.free.at(h, use - 1))
                for c in range(NC):
                    mm = pe.transpose(T[:, c * P:(c + 1) * P], of[:, c * P:(c + 1) * P], eye[:])
                mm.then_inc(T.full.sem, 1)

            def scores(h, t):
                if t == 0:
                    pe.wait_ge(q_moved.sem, q_moved.at(h, 0))
                    pe.wait_ge(k_moved.sem, k_moved.at(h, 0))
                for c in range(2):
                    if S[c].free.due(h, t):
                        pe.wait_ge(S[c].free.sem, S[c].free.at(h, t))
                    pe.matmul(S[c][:], qs[:, c, t * P:(t + 1) * P], ks[:, c, 0, :], start=True, stop=False)
                    pe.matmul(S[c][:], qs[:, c, t * P:(t + 1) * P], ks[:, c, 1, :], start=False,
                              stop=True).then_inc(S[c].full.sem, 1)

            def turn_mix(h, t):
                pe.wait_ge(mixing.sem, mixing.at(h, 4 * (t + 1)))
                turn(h, 3 + t, mix)

            def values(h, use, vals, probsT):
                if O.free.due(h, use - 1):
                    pe.wait_ge(O.free.sem, O.free.at(h, use - 1))
                for c in range(NC):
                    mm = pe.matmul(O[:], vals[:, c, :], probsT[:, c, :], start=c == 0, stop=c == NC - 1)
                mm.then_inc(O.full.sem, 1)

            def sum_squares(h, use, n):
                pe.wait_ge(T.free.sem, T.free.at(h, use - 1))
                pe.wait_ge(squared.sem, squared.at(h, n))
                pe.matmul(T[:], ones, sq[:], start=True, stop=True).then_inc(T.full.sem, 1)

            def out_tiles(h, js):
                pe.wait_ge(y_hg.sem, y_hg.at(h, 3))
                pe.wait_ge(y_da.sem, y_da.at(h, 0))
                pe.wait_ge(o_low.sem, o_low.at(h, 0))
                for j in js:
                    bank, use = (W, j // 2 + 1) if j % 2 == 0 else (O, j // 2 + 2)
                    pe.wait_ge(bank.free.sem, bank.free.at(h, use - 1))
                    for m in range(2):
                        mm = split_product(pe, bank[:], o_hi[:, m, j * P:(j + 1) * P], o_lo[:, m, j * P:(j + 1) * P],
                                           y[:, m, 0], y[:, m, 1], m == 0, m == 1)
                    mm.then_inc(bank.full.sem, 1)

            def diagonal(h):
                pe.wait_ge(key_both.sem, key_both.at(h, 1))
                pe.wait_ge(PB[0].free.sem, PB[0].free.at(h, 2))
                pe.wait_ge(S[0].free.sem, S[0].free.at(h, 4))
                for c in range(NC):
                    mm = pe.matmul(S[0][:, c * P:(c + 1) * P], key_sum[:, c * P:(c + 1) * P],
                                   query[:, c * P:(c + 1) * P], start=True, stop=True)
                mm.then_inc(S[0].full.sem, 1)

            def far(h, x):
                qf, kf, qb, kb = (scaled[:, 0, 0], scaled[:, 0, 1], scaled[:, 1, 0], scaled[:, 1, 1])
                at = lambda a, i, w=1: a[:, i * P:(i + w) * P]
                jobs = {1: (S[1], 5, [(0, at(kf, 0), at(qf, 0)), (1, at(kf, 3), at(qf, 1, 2)), (3, at(kf, 2), at(qf, 3))]),
                        2: (S[0], 6, [(0, at(kf, 1), at(qf, 1, 2)), (2, at(kb, 1), at(qb, 0, 2))]),
                        3: (S[1], 6, [(0, at(kb, 3), at(qb, 0, 2)), (2, at(kb, 2), at(qb, 2)), (3, at(kb, 0), at(qb, 3))])}
                bank, use, products = jobs[x]
                pe.wait_ge(far_scaled.sem, far_scaled.at(h, 10))
                pe.wait_ge(bank.free.sem, bank.free.at(h, use - 1))
                for col, key, qry in products:
                    mm = pe.matmul(bank[:, col * P:col * P + qry.shape[1]], key, qry, start=True, stop=True)
                mm.then_inc(bank.full.sem, 1)

            def near_level(h, l):
                pe.wait_ge(near_scaled.sem, near_scaled.at(h, 3 * (l + 1)))
                pe.wait_ge(S[l % 2].free.sem, S[l % 2].free.at(h, 7 + l // 2 - 1))
                for c in range(NC):
                    mm = pe.matmul(S[l % 2][:, c * P:(c + 1) * P], scaled[:, l % 2, 0, c * P:(c + 1) * P],
                                   scaled[:, l % 2, 1, c * P:(c + 1) * P], start=True, stop=True)
                mm.then_inc(S[l % 2].full.sem, 1)

            def recurrence_values(h):
                pe.wait_ge(S[0].free.sem, S[0].free.at(h, 0))
                pe.wait_ge(S[1].free.sem, S[1].free.at(h, 0))
                pe.wait_ge(far_kept.sem, far_kept.at(h, 0))
                pe.wait_ge(T.free.sem, T.free.at(h, -6))
                values(h, 1, vh, att)

            pe.wait_ge(w_low.sem, w_low.at(0, 0))
            nrm.project(pe, [(w_hi[:, s], w_lo[:, s]) for s in range(3)], PB)
            pe.wait_ge(PB[2].free.sem, PB[2].free.at(0, 0))
            turn(0, 1, vt)
            proj(0, 1)

            def iteration(h, first, last):
                proj(h, 2)
                if not first:
                    recurrence_values(h)
                scores(h, 0)
                proj(h, 3)
                if not first:
                    sum_squares(h, 1, 1)
                scores(h, 1)
                proj(h, 4)
                pe.wait_ge(PB[2].free.sem, PB[2].free.at(h, 1))
                turn(h, 2, vt)
                turn_mix(h, 0)
                scores(h, 2)
                proj(h, 5)
                turn_mix(h, 1)
                scores(h, 3)
                if not first:
                    out_tiles(h, range(0, 4))
                turn_mix(h, 2)
                proj(h, 6)
                turn_mix(h, 3)
                if not first:
                    out_tiles(h, range(4, 8))
                diagonal(h)
                pe.wait_ge(T.free.sem, T.free.at(h, 6))
                values(h, 6, v, mixT)
                far(h, 1)
                far(h, 2)
                sum_squares(h, 7, 2)
                far(h, 3)
                if not last:
                    proj(h, 7)
                near_level(h, 0)
                near_level(h, 1)
                if not last:
                    proj(h, 8)
                near_level(h, 2)
                near_level(h, 3)
                if not last:
                    proj(h, 9)
                near_level(h, 4)
                if not last:
                    proj(h, 10)
                near_level(h, 5)
                if not last:
                    pe.wait_ge(PB[2].free.sem, PB[2].free.at(h, 3))
                    turn(h, 8, vt)
                near_level(h, 6)

            iteration(0, True, False)
            with pe.Fori(1, HEADS - 1) as h:
                iteration(h, False, False)
            iteration(HEADS - 1, False, True)
            recurrence_values(HEADS)
            sum_squares(HEADS, 0, 1)
            out_tiles(HEADS, range(8))

        @block.scalar
        def _(act):
            act.preload_act_table_set(EXP_LOG)
            for k in range(KT + 1):
                if k < KT:
                    act.wait_ge(x_turned.sem, x_turned.at(0, k + 1))
                    act.activation(xT[:, k], S[k % 2][:], ACT.Copy).then_inc(x_kept.sem, 1)
                if k >= 1:
                    act.wait_ge(x_kept.sem, x_kept.at(0, k))
                    nrm.square(act, k - 1)

            def high(h, n):
                s = (n + 2) % 3
                act.wait_ge(w_in_sem[s].sem, w_in_sem[s].at(h, (n + 2) // 3))
                bank, use = bank_of(n - 3)
                if bank.full.due(h, use):
                    act.wait_ge(bank.full.sem, bank.full.at(h, use))
                act.activation(w_hi[:, s], w_raw[:, s], ACT.Copy).then_inc(w_high.sem, 1)

            def high_out(h, m):
                act.wait_ge(o_in.sem, o_in.at(h, m + 1))
                if O.full.due(h, 5):
                    act.wait_ge(O.full.sem, O.full.at(h, 5))
                act.activation(o_hi[:, m], o_raw[:], ACT.Copy).then_inc(o_high.sem, 1)

            def soften(h, d):
                bank = PB[d]
                at = soft[:, d]
                act.wait_ge(bank.full.sem, bank.full.at(h, 1))
                if near_scaled.due(h, 0):
                    act.wait_ge(near_scaled.sem, near_scaled.at(h, 0))
                act.activation(at, bank[:], ACT.Abs).then_inc(softplus.sem, 1)
                act.wait_ge(softplus.sem, softplus.at(h, 3 * d + 1))
                act.activation(at, at, ACT.Exp, scale=-1.0).then_inc(softplus.sem, 1)
                act.wait_ge(softplus.sem, softplus.at(h, 3 * d + 2))
                act.activation(at, at, ACT.Ln, bias=1.0).then_inc(softplus.sem, 1)

            def square(h, use, n):
                act.wait_ge(O.full.sem, O.full.at(h, use))
                act.wait_ge(T.full.sem, T.full.at(h, 7 - 8 if n == 1 else 1))
                if squared.due(h, n - 1):
                    act.wait_ge(squared.sem, squared.at(h, n - 1))
                act.activation(sq[:], O[:], ACT.Square).then_inc(squared.sem, 1)

            def root(h, use, n):
                act.wait_ge(T.full.sem, T.full.at(h, use))
                if (y_da if n == 1 else y_hg).due(h, 0 if n == 1 else 1):
                    act.wait_ge((y_da if n == 1 else y_hg).sem, (y_da if n == 1 else y_hg).at(h, 0 if n == 1 else 1))
                act.activation(rstd[:], T[:], ACT.Ln, bias=eps, scale=1.0 / P).then_inc(T.free.sem, 1)
                act.wait_ge(T.free.sem, T.free.at(h, use))
                act.activation(rstd[:], rstd[:], ACT.Exp, scale=-0.5).then_inc(rooted.sem, 1)

            def key(h, d):
                act.wait_ge(PB[d].free.sem, PB[d].free.at(h, 1))
                act.activation(keys[:, d], keys[:, d], ACT.Exp).then_inc(key_exp.sem, 1)

            def soft_max(h, t):
                act.wait_ge(neg_peak.sem, neg_peak.at(h, t + 1))
                if mixing.due(h, 4 * t):
                    act.wait_ge(mixing.sem, mixing.at(h, 4 * t))
                for c in range(2):
                    i = 2 * t + c
                    act.activation(probs[:, c], S[c][:], ACT.Exp, bias=neg_max[:, i:i + 1], scale=SCALE,
                                   accum_out=row_sum[:, i:i + 1]).then_inc(S[c].free.sem, 1)

            def keep_values(h, use, into, out_use):
                act.wait_ge(T.full.sem, T.full.at(h, use))
                if O.full.due(h, out_use):
                    act.wait_ge(O.full.sem, O.full.at(h, out_use))
                act.activation(into[:, :, :].rearrange("p c f -> p (c f)"), T[:], ACT.Copy).then_inc(T.free.sem, 1)

            def keep_mix(h, t):
                act.wait_ge(T.full.sem, T.full.at(h, 3 + t))
                if O.full.due(h, 0):
                    act.wait_ge(O.full.sem, O.full.at(h, 0))
                act.activation(mixT[:, :, t * P:(t + 1) * P], chunked(T[:]), ACT.Copy).then_inc(T.free.sem, 1)

            def silu(h, n, into):
                bank, use = bank_of(n)
                act.wait_ge(bank.full.sem, bank.full.at(h, use))
                act.activation(into[:], bank[:], ACT.Silu).then_inc(bank.free.sem, 1)

            def far_decays(h):
                act.wait_ge(summed.sem, summed.at(h, 2 * NC))
                if far_scaled.due(h, 0):
                    act.wait_ge(far_scaled.sem, far_scaled.at(h, 0))
                act.activation(total[:, 0], gf[:, :, P], ACT.Exp).then_inc(far_exp.sem, 1)
                act.activation(total[:, 1], gb[:, :, P], ACT.Exp).then_inc(far_exp.sem, 1)
                act.wait_ge(log_f.sem, log_f.at(h, 2))
                act.activation(chunked(soft[:, 0, 0:3 * P]), gf[:, 1:NC, 1:LP], ACT.Exp).then_inc(far_exp.sem, 1)
                act.activation(chunked(soft[:, 1, 0:3 * P]), gb[:, 1:NC, 0:P], ACT.Exp).then_inc(far_exp.sem, 1)
                act.wait_ge(far_diff.sem, far_diff.at(h, 2))
                flat = decay[:, :, :].rearrange("p a t -> p (a t)")[:, 0:6 * P]
                act.activation(flat, flat, ACT.Exp).then_inc(far_exp.sem, 1)

            def keep_far(h, x):
                if x == 1:
                    if O.full.due(h, 1):
                        act.wait_ge(O.full.sem, O.full.at(h, 1))
                jobs = {1: (S[1], 5, (0, 1, 4, 0), (2, 3, 4, 3)),
                        2: (S[0], 6, (1, 2, 4, 0), (2, 0, 2, 2)),
                        3: (S[1], 6, (3, 0, 3, 0), (1, 0, 1, 3))}
                bank, use, one, two = jobs[x]
                act.wait_ge(bank.full.sem, bank.full.at(h, use))
                for (s, t0, t1, col), count in ((one, far_kept), (two, bank.free)):
                    act.activation(att[:, s, t0 * P:t1 * P], bank[:, col * P:(col + t1 - t0) * P],
                                   ACT.Copy).then_inc(count.sem, 1)

            def near_decays(h, l):
                act.wait_ge(near_fwd.sem, near_fwd.at(h, 2 * (l + 1)))
                act.wait_ge(near_bwd.sem, near_bwd.at(h, 2 * (l + 1)))
                flat = buf(l)[:, :, :].rearrange("p a t -> p (a t)")
                act.activation(flat, flat, ACT.Exp).then_inc(near_exp.sem, 1)

            def keep_vt(h, n, turned_use):
                bank, use = bank_of(n)
                act.wait_ge(bank.full.sem, bank.full.at(h, use))
                if T.full.due(h, turned_use):
                    act.wait_ge(T.full.sem, T.full.at(h, turned_use))
                act.activation(vt[:], bank[:], ACT.Copy).then_inc(bank.free.sem, 1)

            high(0, -2)
            high(0, -1)
            act.wait_ge(ready.sem, ready.at(0, 4))
            nrm.root(act)
            high(0, 0)
            nrm.highs(act)
            act.wait_ge(lam_steps.sem, lam_steps.at(0, 2))
            act.activation(lam_e, lam_e, ACT.Exp).then_inc(lam_steps.sem, 1)
            high(0, 1)
            high(0, 2)
            keep_vt(0, 0, 0)
            act.wait_ge(T.full.sem, T.full.at(0, 1))
            act.activation(v[:, :, :].rearrange("p c f -> p (c f)"), T[:], ACT.Copy).then_inc(T.free.sem, 1)

            def iteration(h, first, last):
                high(h, 3)
                soften(h, 0)
                high(h, 4)
                soften(h, 1)
                if not first:
                    square(h, 1, 1)
                key(h, 0)
                soft_max(h, 0)
                high(h, 5)
                key(h, 1)
                if not first:
                    root(h, 1, 1)
                keep_vt(h, 3, 1 if first else 0)
                soft_max(h, 1)
                high(h, 6)
                keep_values(h, 2, vh, 1)
                keep_mix(h, 0)
                soft_max(h, 2)
                if not last:
                    high(h, 7)
                keep_mix(h, 1)
                soft_max(h, 3)
                if not last:
                    high(h, 8)
                silu(h, 4, query)
                silu(h, 5, gate_h)
                keep_mix(h, 2)
                silu(h, 6, gate_a)
                act.preload_act_table_set(EXP_LOG)
                keep_mix(h, 3)
                far_decays(h)
                high_out(h, 0)
                if not last:
                    high(h, 9)
                square(h, 6, 2)
                keep_far(h, 1)
                near_decays(h, 0)
                near_decays(h, 1)
                keep_far(h, 2)
                keep_far(h, 3)
                root(h, 7, 2)
                near_decays(h, 2)
                near_decays(h, 3)
                if not last:
                    high(h, 10)
                near_decays(h, 4)
                if not last:
                    high(h, 11)
                near_decays(h, 5)
                if not last:
                    keep_vt(h, 9, 2)
                near_decays(h, 6)
                high_out(h, 1)
                if not last:
                    keep_values(h, 8, v, 6)

            iteration(0, True, False)
            with act.Fori(1, HEADS - 1) as h:
                iteration(h, False, False)
            iteration(HEADS - 1, False, True)
            square(HEADS, 1, 1)
            root(HEADS, 0, 1)

        @block.vector
        def _(dve):
            dve.sem_inc(O.free.sem, 1)
            dve.sem_inc(W.free.sem, 1)
            for at, value in ((ones, 1.0), (eps, EPS), (gf[:, :, 0:1], 0.0), (gb[:, :, 0:1], 0.0)):
                dve.memset(at, value).then_inc(ready.sem, 1)
            dve.wait_ge(landed.sem, landed.at(0, 6))
            dve.tensor_copy(level_mask[:], mask_raw).then_inc(ready.sem, 1)
            pairs = yn[:, 0:4 * HD].rearrange("p (a c d) -> p a c d", a=2, c=2)
            prod = yn[:, 4 * HD:6 * HD].rearrange("p (a d) -> p a d", a=2)
            dve.tensor_tensor(prod, pairs[:, :, 0, :], pairs[:, :, 1, :], ALU.mult).then_inc(lam_steps.sem, 1)
            dve.wait_ge(lam_steps.sem, lam_steps.at(0, 1))
            dve.tensor_reduce(lam_e, prod, AX_X, ALU.add).then_inc(lam_steps.sem, 1)
            nrm.add(dve)
            nrm.scale(dve)
            dve.wait_ge(lam_steps.sem, lam_steps.at(0, 3))
            dve.tensor_tensor(lam_t, lam_e[:, 0:1], lam_e[:, 1:2], ALU.subtract).then_inc(lam_steps.sem, 1)
            dve.wait_ge(lam_steps.sem, lam_steps.at(0, 4))
            dve.tensor_scalar(lam_t, lam_t, LAM_INIT, None, ALU.add).then_inc(lam_steps.sem, 1)
            dve.wait_ge(lam_steps.sem, lam_steps.at(0, 5))
            dve.wait_ge(ready.sem, ready.at(0, 5))

            def gates(h, d):
                bank, g = PB[d], (gf, gb)[d]
                dve.wait_ge(softplus.sem, softplus.at(h, 3 * d + 3))
                if summed.due(h, NC * d):
                    dve.wait_ge(summed.sem, summed.at(h, NC * d))
                dve.scalar_tensor_tensor(out=lf[:], in0=bank[:], scalar=0.0, in1=soft[:, d], op0=ALU.min,
                                         op1=ALU.subtract).then_inc(log_f.sem, 1)
                dve.wait_ge(log_f.sem, log_f.at(h, d + 1))
                if near_scaled.due(h, 0):
                    dve.wait_ge(near_scaled.sem, near_scaled.at(h, 0))
                dve.tensor_tensor(keys[:, d], lf[:], bank[:], ALU.subtract).then_inc(bank.free.sem, 1)
                if near_bwd.due(h, 0):
                    dve.wait_ge(near_bwd.sem, near_bwd.at(h, 0))
                if near_fwd.due(h, 0):
                    dve.wait_ge(near_fwd.sem, near_fwd.at(h, 0))
                for c in range(NC):
                    dve.tensor_tensor_scan(g[:, c, 1:LP], ones, lf[:, c * P:(c + 1) * P], 0.0, ALU.mult,
                                           ALU.add).then_inc(summed.sem, 1)

            def maxima(h, t):
                if neg_peak.due(h, t):
                    dve.wait_ge(neg_peak.sem, neg_peak.at(h, t))
                for c in range(2):
                    i = 2 * t + c
                    dve.wait_ge(S[c].full.sem, S[c].full.at(h, t + 1))
                    dve.tensor_reduce(row_max[:, i:i + 1], S[c][:], AX_X, ALU.max).then_inc(peak.sem, 1)
                dve.wait_ge(peak.sem, peak.at(h, 2 * t + 2))
                dve.tensor_scalar(neg_max[:, 2 * t:2 * t + 2], row_max[:, 2 * t:2 * t + 2], -SCALE, None,
                                  ALU.mult).then_inc(neg_peak.sem, 1)

            def mixes(h, t):
                a, b = weight[:, 2 * t:2 * t + 1], weight[:, 2 * t + 1:2 * t + 2]
                dve.wait_ge(S[0].free.sem, S[0].free.at(h, t + 1))
                dve.wait_ge(S[1].free.sem, S[1].free.at(h, t + 1))
                if mixing.due(h, 4 * t):
                    dve.wait_ge(mixing.sem, mixing.at(h, 4 * t))
                dve.reciprocal(weight[:, 2 * t:2 * t + 2], row_sum[:, 2 * t:2 * t + 2]).then_inc(mixing.sem, 1)
                dve.wait_ge(mixing.sem, mixing.at(h, 4 * t + 1))
                dve.tensor_tensor(b, b, lam_t, ALU.mult).then_inc(mixing.sem, 1)
                dve.wait_ge(mixing.sem, mixing.at(h, 4 * t + 2))
                dve.tensor_scalar(probs[:, 1], probs[:, 1], b, None, ALU.mult).then_inc(mixing.sem, 1)
                dve.wait_ge(mixing.sem, mixing.at(h, 4 * t + 3))
                turned_use = 2 + t if t else -2
                if T.full.due(h, turned_use):
                    dve.wait_ge(T.full.sem, T.full.at(h, turned_use))
                dve.scalar_tensor_tensor(out=mix[:], in0=probs[:, 0], scalar=a, in1=probs[:, 1], op0=ALU.mult,
                                         op1=ALU.subtract).then_inc(mixing.sem, 1)

            def add_out(h, js):
                for j in js:
                    bank, use = (W, j // 2 + 1) if j % 2 == 0 else (O, j // 2 + 2)
                    dve.wait_ge(bank.full.sem, bank.full.at(h, use))
                    dve.wait_ge((W if j % 2 == 0 else O).free.sem, (W if j % 2 == 0 else O).free.at(h, use - 1))
                    dve.tensor_tensor(xT[:, j], xT[:, j], bank[:], ALU.add).then_inc(bank.free.sem, 1)

            def outputs(h, m):
                use, n, w, gate, count, factor = ((1, 1, w_hg, gate_h, y_hg, 1.0) if m else
                                                  (6, 2, w_sub, gate_a, y_da, 1.0 - LAM_INIT))
                dve.wait_ge(rooted.sem, rooted.at(h, n))
                if (y_da if m else y_hg).due(h, 0 if m else 3):
                    dve.wait_ge((y_da if m else y_hg).sem, (y_da if m else y_hg).at(h, 0 if m else 3))
                dve.scalar_tensor_tensor(out=yn[:], in0=O[:], scalar=w[:, 0:1], in1=rstd[:], op0=ALU.mult,
                                         op1=ALU.mult).then_inc(O.free.sem, 1)
                dve.wait_ge(O.free.sem, O.free.at(h, use))
                bank, gate_use = bank_of(5 if m else 6)
                dve.wait_ge(bank.free.sem, bank.free.at(h, gate_use - (3 if m else 0)))
                dve.scalar_tensor_tensor(out=yn[:], in0=yn[:], scalar=factor, in1=gate[:], op0=ALU.mult,
                                         op1=ALU.mult).then_inc(count.sem, 1)
                dve.wait_ge(count.sem, count.at(h, 1))
                if O.full.due(h, -1 if m else 5):
                    dve.wait_ge(O.full.sem, O.full.at(h, -1 if m else 5))
                dve.tensor_copy(y[:, m, 0], yn[:]).then_inc(count.sem, 1)
                dve.wait_ge(count.sem, count.at(h, 2))
                dve.tensor_tensor(y[:, m, 1], yn[:], y[:, m, 0].bitcast(F32), ALU.subtract).then_inc(count.sem, 1)

            def rotate(h, n):
                bank, use = bank_of(n)
                i = 0 if n == 7 else 5
                dve.wait_ge(bank.full.sem, bank.full.at(h, use))
                if roped.due(h, i):
                    dve.wait_ge(roped.sem, roped.at(h, i))
                dve.tensor_tensor(turned[:, 0], bank[:], rope[:, 0], ALU.mult).then_inc(roped.sem, 1)
                dve.stream_shuffle(turned[:, 1], bank[:], SWAP).then_inc(bank.free.sem, 1)
                dve.wait_ge(bank.free.sem, bank.free.at(h, use))
                dve.tensor_tensor(turned[:, 1], turned[:, 1], rope[:, 1], ALU.mult).then_inc(roped.sem, 1)
                dve.wait_ge(roped.sem, roped.at(h, i + 2))
                dve.tensor_tensor(turned[:, 0], turned[:, 0], turned[:, 1], ALU.add).then_inc(roped.sem, 1)
                dve.wait_ge(roped.sem, roped.at(h, i + 3))
                if (k_moved if n == 7 else q_moved).due(h, 0 if n == 7 else 4):
                    dve.wait_ge((k_moved if n == 7 else q_moved).sem, (k_moved if n == 7 else q_moved).at(h, 0 if n == 7 else 4))
                dve.tensor_copy(parts[:, 0], turned[:, 0]).then_inc(roped.sem, 1)
                dve.wait_ge(roped.sem, roped.at(h, i + 4))
                dve.tensor_tensor(parts[:, 1], turned[:, 0], parts[:, 0].bitcast(F32),
                                  ALU.subtract).then_inc(roped.sem, 1)

            def far_differences(h):
                if near_scaled.due(h, 0):
                    dve.wait_ge(near_scaled.sem, near_scaled.at(h, 0))
                edge = lambda g: g[:, 0:3, P:LP].broadcast_to([P, 3, P])
                flat = decay[:, :, :].rearrange("p a t -> p (a t)")
                dve.wait_ge(summed.sem, summed.at(h, 2 * NC))
                dve.tensor_tensor(chunked(flat[:, 0:3 * P]), edge(gf), gf[:, 0:3, 1:LP],
                                  ALU.subtract).then_inc(far_diff.sem, 1)
                dve.tensor_tensor(chunked(flat[:, 3 * P:6 * P]), edge(gb), gb[:, 0:3, 0:P],
                                  ALU.subtract).then_inc(far_diff.sem, 1)

            def both_keys(h):
                dve.wait_ge(key_exp.sem, key_exp.at(h, 2))
                if S[0].full.due(h, -5):
                    dve.wait_ge(S[0].full.sem, S[0].full.at(h, -5))
                dve.tensor_tensor(key_sum, keys[:, 0], keys[:, 1], ALU.add).then_inc(key_both.sem, 1)

            def place_diagonal(h):
                dve.wait_ge(S[0].full.sem, S[0].full.at(h, 5))
                if O.full.due(h, 1):
                    dve.wait_ge(O.full.sem, O.full.at(h, 1))
                dve.tensor_tensor(att_diag, chunked(S[0][:]), eye[:].unsqueeze(1).broadcast_to([P, NC, P]),
                                  ALU.mult).then_inc(S[0].free.sem, 1)

            def far_scale(h):
                qf, kf, qb, kb = (scaled[:, 0, 0], scaled[:, 0, 1], scaled[:, 1, 0], scaled[:, 1, 1])
                flat = decay[:, :, :].rearrange("p a t -> p (a t)")
                from_f, from_b = soft[:, 0], soft[:, 1]
                dve.wait_ge(far_exp.sem, far_exp.at(h, 5))
                dve.wait_ge(PB[0].free.sem, PB[0].free.at(h, 2))
                if S[0].full.due(h, 0):
                    dve.wait_ge(S[0].full.sem, S[0].full.at(h, 0))
                mul = lambda out, a, b: dve.tensor_tensor(out, a, b, ALU.mult).then_inc(far_scaled.sem, 1)
                by = lambda out, a, s: dve.tensor_scalar(out, a, s, None, ALU.mult).then_inc(far_scaled.sem, 1)
                mul(qf[:, 0:2 * P], query[:, P:3 * P], from_f[:, 0:2 * P])
                mul(qf[:, 3 * P:4 * P], query[:, 3 * P:4 * P], from_f[:, 2 * P:3 * P])
                mul(kf[:, 0:3 * P], keys[:, 0, 0:3 * P], flat[:, 0:3 * P])
                mul(kb[:, 0:3 * P], keys[:, 1, P:4 * P], from_b[:, 0:3 * P])
                mul(qb[:, P:3 * P], query[:, P:3 * P], flat[:, 4 * P:6 * P])
                mul(qb[:, 3 * P:4 * P], query[:, 0:P], flat[:, 3 * P:4 * P])
                dve.wait_ge(far_scaled.sem, far_scaled.at(h, 6))
                by(qf[:, 2 * P:3 * P], qf[:, 3 * P:4 * P], total[:, 0, 2:3])
                by(kf[:, 3 * P:4 * P], kf[:, 0:P], total[:, 0, 1:2])
                by(qb[:, 0:P], qb[:, 3 * P:4 * P], total[:, 1, 1:2])
                by(kb[:, 3 * P:4 * P], kb[:, 2 * P:3 * P], total[:, 1, 2:3])

            def near_differences(h, l):
                if l < 2:
                    dve.wait_ge(far_scaled.sem, far_scaled.at(h, 10))
                else:
                    dve.wait_ge(near_scaled.sem, near_scaled.at(h, 3 * (l - 1)))
                left, right = near(gf[:, :, :], l, 1)
                key_left, _ = near(buf(l)[:, 0], l)
                _, query_right = near(buf(l)[:, 1], l)
                mid = middle(gf, l)
                dve.tensor_tensor(key_left, mid, left, ALU.subtract).then_inc(near_fwd.sem, 1)
                dve.tensor_tensor(query_right, right, mid, ALU.subtract).then_inc(near_fwd.sem, 1)

            def near_scale(h, l):
                b = 1 << l
                halves = lambda ap, i: ap.rearrange("p (n h b) -> p n h b", h=2, b=b)[:, :, i, :]
                dve.wait_ge(near_exp.sem, near_exp.at(h, l + 1))
                if l < 2:
                    dve.wait_ge(S[1].full.sem, S[1].full.at(h, 6))
                else:
                    dve.wait_ge(S[l % 2].full.sem, S[l % 2].full.at(h, 6 + l // 2))
                for i in range(2):
                    dve.tensor_tensor(halves(scaled[:, l % 2, 0], i), halves(keys[:, i], i), halves(buf(l)[:, 0], i),
                                      ALU.mult).then_inc(near_scaled.sem, 1)
                dve.tensor_tensor(scaled[:, l % 2, 1], query[:], buf(l)[:, 1], ALU.mult).then_inc(near_scaled.sem, 1)

            def place_level(h, l):
                bank = S[l % 2]
                dve.wait_ge(bank.full.sem, bank.full.at(h, 7 + l // 2))
                if l == 0:
                    dve.wait_ge(S[0].free.sem, S[0].free.at(h, 5))
                else:
                    dve.wait_ge(S[(l - 1) % 2].free.sem, S[(l - 1) % 2].free.at(h, 7 + (l - 1) // 2))
                dve.sem_inc(place_go.sem, 1)
                dve.copy_predicated(att_diag, level_mask[:, l].unsqueeze(1).broadcast_to([P, NC, P]),
                                    chunked(bank[:])).then_inc(bank.free.sem, 1)

            rotate(-1, 7)
            rotate(-1, 8)

            def iteration(h, first, last):
                gates(h, 0)
                gates(h, 1)
                maxima(h, 0)
                mixes(h, 0)
                maxima(h, 1)
                if not first:
                    outputs(h, 1)
                far_differences(h)
                mixes(h, 1)
                maxima(h, 2)
                both_keys(h)
                mixes(h, 2)
                maxima(h, 3)
                if not first:
                    add_out(h, range(0, 4))
                mixes(h, 3)
                if not first:
                    add_out(h, range(4, 8))
                far_scale(h)
                near_differences(h, 0)
                near_differences(h, 1)
                place_diagonal(h)
                near_scale(h, 0)
                near_differences(h, 2)
                near_scale(h, 1)
                near_differences(h, 3)
                outputs(h, 0)
                near_scale(h, 2)
                near_differences(h, 4)
                place_level(h, 0)
                near_scale(h, 3)
                near_differences(h, 5)
                place_level(h, 1)
                if not last:
                    rotate(h, 7)
                near_scale(h, 4)
                near_differences(h, 6)
                place_level(h, 2)
                near_scale(h, 5)
                place_level(h, 3)
                if not last:
                    rotate(h, 8)
                place_level(h, 4)
                near_scale(h, 6)
                place_level(h, 5)
                place_level(h, 6)

            iteration(0, True, False)
            with dve.Fori(1, HEADS - 1) as h:
                iteration(h, False, False)
            iteration(HEADS - 1, False, True)
            outputs(HEADS, 1)
            add_out(HEADS, range(8))

        @block.gpsimd
        def _(pool):
            def low(h, n):
                s = (n + 2) % 3
                pool.wait_ge(w_high.sem, w_high.at(h, n))
                pool.tensor_tensor(w_lo[:, s], w_raw[:, s], w_hi[:, s].bitcast(F32),
                                   ALU.subtract).then_inc(w_low.sem, 1)

            def low_out(h, m):
                pool.wait_ge(o_high.sem, o_high.at(h, m + 1))
                pool.tensor_tensor(o_lo[:, m], o_raw[:], o_hi[:, m].bitcast(F32),
                                   ALU.subtract).then_inc(o_low.sem, 1)

            def near_differences(h, l):
                if l < 2:
                    pool.wait_ge(far_scaled.sem, far_scaled.at(h, 10))
                else:
                    pool.wait_ge(near_scaled.sem, near_scaled.at(h, 3 * (l - 1)))
                left, right = near(gb[:, :, :], l, 0)
                _, key_right = near(buf(l)[:, 0], l)
                query_left, _ = near(buf(l)[:, 1], l)
                mid = middle(gb, l)
                pool.tensor_tensor(key_right, right, mid, ALU.subtract).then_inc(near_bwd.sem, 1)
                pool.tensor_tensor(query_left, mid, left, ALU.subtract).then_inc(near_bwd.sem, 1)

            for n in (-2, -1, 0, 1, 2):
                low(0, n)

            def iteration(h, last):
                for n in range(3, 7 if last else 9):
                    low(h, n)
                near_differences(h, 0)
                near_differences(h, 1)
                if not last:
                    low(h, 9)
                near_differences(h, 2)
                near_differences(h, 3)
                low_out(h, 0)
                near_differences(h, 4)
                if not last:
                    low(h, 10)
                near_differences(h, 5)
                if not last:
                    low(h, 11)
                near_differences(h, 6)
                low_out(h, 1)

            iteration(0, False)
            with pool.Fori(1, HEADS - 1) as h:
                iteration(h, False)
            iteration(HEADS - 1, True)


def odd_layer(nc, xT, eye, ones, rope, eps, w_in, w_out, norm, norm_out, sink_d, band_d, out):
    with ExitStack() as ctx:
        sb = lambda name, shape, dt=F32: ctx.enter_context(nc.sbuf_tensor(name, shape, dt))
        sem = lambda name, *a, **k: Count(ctx.enter_context(nc.semaphore(name)), *a, **k)
        SLOTS = 4

        hH, hL = sb("hH2", [P, KT, SEQ], F32R), sb("hL2", [P, KT, SEQ], F32R)
        w_raw = sb("w_raw2", [P, SLOTS, KT, P])
        w_hi, w_lo = sb("w_hi2", [P, SLOTS, KT, P], F32R), sb("w_lo2", [P, SLOTS, KT, P], F32R)
        o_raw = sb("o_raw2", [P, DM])
        o_hi, o_lo = sb("o_hi2", [P, 2, DM], F32R), sb("o_lo2", [P, 2, DM], F32R)
        y = sb("y2", [P, 2, 2, SEQ], F32R)
        parts = sb("parts2", [P, 2, SEQ], F32R)
        qs = sb("qs2", [P, 2, 2, SEQ], F32R)
        ks = sb("ks2", [P, 4 * 2 * SEQ], F32R)
        v = sb("v2", [P, NC, 4 * HD])
        probs = sb("probs2", [P, 2, 2, 3 * P])
        probsT = sb("probsT", [P, 2, 2, 3 * P])
        normed = sb("normed", [P, SEQ])
        gate = sb("gate2", [P, 2, SEQ])
        gated = sb("gated", [P, 2, SEQ])
        vt = sb("vt2", [P, SEQ])
        turned = sb("turned2", [P, 2, SEQ])
        soft = sb("soft2", [P, 2, SEQ])
        rstd = sb("rstd2", [P, SEQ])
        small = sb("small2", [P, 64])
        sink, neg_sink = sb("sink", [P, 2 * PAIRS]), sb("neg_sink", [P, 2 * PAIRS])
        wn = sb("wn2", [P, KT])
        row_squares, row_rstd = sb("row_squares", [P, NC, 2]), sb("row_rstd", [P, NC])
        band_raw = sb("band_raw", [P, 2, P])
        band, eye_b = sb("band", [P, 2, P], BF16), sb("eye_b", [P, P], BF16)
        w_final = soft[:, :, :].rearrange("p a t -> p (a t)")
        rows = w_raw[:, :, :, :].rearrange("p s k c -> p s (k c)")

        row_max, neg_max = small[:, 0:16], small[:, 16:32]
        row_sum, weight = small[:, 32:48], small[:, 48:64]

        PB = [Bank(nc, ctx, f"odd_proj{b}", 2, 3) for b in range(2)]
        S = [Bank(nc, ctx, f"odd_score{a}", 8) for a in range(2)]
        T = [Bank(nc, ctx, f"odd_turn{a}", 8) for a in range(2)]
        O, W = Bank(nc, ctx, "odd_out", 2), Bank(nc, ctx, "odd_wide", 10, -9)

        ready, landed = sem("odd_constants_ready"), sem("odd_constants_landed", unit=DMA)
        w_in_sem = [sem(f"odd_weights{i}_landed", 1, 1 + i // 2, unit=DMA) for i in range(SLOTS)]
        load_go = sem("odd_load_go")
        w_high, w_low = sem("odd_weights_high", 4, 6), sem("odd_weights_low", 4, 6)
        o_in = sem("odd_out_weights_landed", 2, 0, unit=DMA)
        o_high, o_low = sem("odd_out_weights_high", 2), sem("odd_out_weights_low", 2)
        peak, neg_peak = sem("odd_row_max", 16), sem("odd_neg_row_max", 8)
        roped = sem("odd_roped", 10, 15)
        k_moved, q_moved = sem("odd_k_moved", unit=DMA), sem("odd_q_moved", 8, 4, unit=DMA)
        v_turned, v_kept = sem("odd_v_turned"), sem("odd_v_kept")
        sink_shift, sink_exp = sem("sink_shifted", 2), sem("sink_exp", 2)
        weighed = sem("weighed", 4)
        split = sem("odd_y_split", 4, -2)
        turned_back = [sem("features0_511_turned"), sem("features512_1023_turned")]
        row_squared, row_rooted, kept = sem("rows_squared"), sem("rows_rooted"), sem("rows_kept")
        final_landed, stores = sem("final_norm_landed", unit=DMA), sem("stored", unit=DMA)
        nrm = Norm(nc, ctx, "norm_odd", xT, wn, ones, eps, (turned[:, 0], turned[:, 1], gated[:, 0], gated[:, 1]),
                   soft, rstd[:], O, hH, hL)
        row_banks = [(S[0], O), (S[1], W), (T[0], PB[0]), (T[1], PB[1])]

        w_cols = w_in.rearrange("(k p) n -> p k n", p=P)

        def bank_of(n):
            return PB[(n - 1) % 2], (n - 1) // 2 + 1


        def key_head(h, half):
            return 2 * half + h // 4

        def window(t):
            lo, hi = max(0, t - 1), min(NC - 1, t + 1)
            return lo, hi - lo + 1

        def tile_use(half, t):
            return NC * half + t + 1

        def turn_of(half, steady):
            return 5 * half + 1 if steady else 10

        block = ctx.enter_context(nc.Block())

        @block.sync
        def _(sp):
            sp.dma_start(sink[:], sink_d.broadcast_to([P, 2 * PAIRS])).then_inc(landed.sem, DMA)
            for to, of in ((wn, norm), (band_raw, band_d)):
                sp.dma_start(to[:], of).then_inc(landed.sem, DMA)

            def load(h, n):
                if w_low.due(h, n - SLOTS):
                    sp.wait_ge(w_low.sem, w_low.at(h, n - SLOTS))
                sp.sem_inc(load_go.sem, 1)
                gates = DI + 4 * P
                if n <= 0:
                    col = {-5: DI, -3: DI + P, -4: DI + 2 * P, -2: DI + 3 * P, -1: 0, 0: gates}[n]
                else:
                    col = (KT * P, gates + KT * P, P, gates + P)[(n - 1) % 4] + (h + (n - 1) // 4) * P
                s = (n + 3) % SLOTS
                sp.dma_start(w_raw[:, s], w_cols[:, :, bass.ds(col, P)]).then_inc(w_in_sem[s].sem, DMA)

            def load_out(h, m):
                if o_low.due(h, m):
                    sp.wait_ge(o_low.sem, o_low.at(h, m))
                sp.sem_inc(load_go.sem, 1)
                row = m * DM + h * P
                sp.dma_start(o_raw[:], w_out[bass.ds(row, P), :]).then_inc(o_in.sem, DMA)

            def load_last(m):
                s, n = 2 + m, 3 + m
                sp.wait_ge(w_low.sem, w_low.at(HEADS - 1, n - SLOTS))
                row = m * DM + (HEADS - 1) * P
                sp.dma_start(w_raw[:, s].rearrange("p k c -> p (k c)"),
                             w_out[row:row + P, :]).then_inc(w_in_sem[s].sem, DMA)

            def move_q(h, half, roped_to):
                sp.wait_ge(roped.sem, roped.at(h, roped_to))
                for c in range(2):
                    for i in range(2):
                        sp.dma_start(qs[HD * i:HD * i + HD, half, c, :].bitcast(F32),
                                     parts[HD * c:HD * c + HD, i, :].bitcast(F32)).then_inc(q_moved.sem, DMA)

            def move_k(g, roped_to):
                sp.wait_ge(roped.sem, roped.at(0, roped_to))
                for c in range(2):
                    to = ks[:, (2 * g + c) * 2 * SEQ:(2 * g + c + 1) * 2 * SEQ].rearrange("p (i t) -> p i t", i=2)
                    for i in range(2):
                        sp.dma_start(to[HD * i:HD * i + HD].bitcast(F32),
                                     parts[HD * c:HD * c + HD, :, :].bitcast(F32)).then_inc(k_moved.sem, DMA)

            for n in range(-5, 1):
                load(0, n)
            load(0, 1)
            load(0, 2)
            move_k(0, -10)
            move_k(1, -5)
            move_q(0, 0, 0)

            def iteration(h, zeroth, last):
                for n in (3, 4):
                    if last:
                        load_last(n - 3)
                    else:
                        load(h, n)
                if not zeroth:
                    load_out(h - 1, 1)
                if S[1].full.due(h, 0):
                    sp.wait_ge(S[1].full.sem, S[1].full.at(h, 0))
                sp.sem_inc(load_go.sem, 1)
                move_q(h, 1, 5)
                if not last:
                    load_out(h, 0)
                    load(h, 5)
                    load(h, 6)
                    sp.wait_ge(S[1].full.sem, S[1].full.at(h, tile_use(0, 3)))
                    sp.sem_inc(load_go.sem, 1)
                    move_q(h, 0, 10)

            iteration(0, True, False)
            with sp.Fori(1, HEADS - 1) as h:
                iteration(h, False, False)
            iteration(HEADS - 1, False, True)
            sp.wait_ge(nrm.high.sem, nrm.high.at(0, KT))
            sp.wait_ge(nrm.low.sem, nrm.low.at(0, KT))
            sp.dma_start(w_final, norm_out.broadcast_to([P, DM])).then_inc(final_landed.sem, DMA)
            for t in range(NC):
                sp.wait_ge(kept.sem, kept.at(0, 2 * t + 2))
                sp.dma_start(out[t * P:(t + 1) * P, :], rows[:, t]).then_inc(stores.sem, DMA)
            sp.wait_ge(stores.sem, stores.at(0, NC))

        @block.tensor
        def _(pe):
            def proj(h, n, half=None):
                bank, use = bank_of(n)
                if half != 1:
                    pe.wait_ge(w_low.sem, w_low.at(h, n))
                    if bank.free.due(h, use - 1):
                        pe.wait_ge(bank.free.sem, bank.free.at(h, use - 1))
                s = (n + 3) % SLOTS
                tiles = range(KT) if half is None else range(half * KT // 2, (half + 1) * KT // 2)
                for k in tiles:
                    mm = split_product(pe, bank[:], w_hi[:, s, k], w_lo[:, s, k], hH[:, k], hL[:, k],
                                       k == 0, k == KT - 1)
                if half != 0:
                    mm.then_inc(bank.full.sem, 1)

            def scores(h, half, t):
                lo, n = window(t)
                if t == 0:
                    pe.wait_ge(q_moved.sem, q_moved.at(h, 4 * half))
                for a in range(2):
                    if S[a].free.due(h, tile_use(half, t) - 1):
                        pe.wait_ge(S[a].free.sem, S[a].free.at(h, tile_use(half, t) - 1))
                    at, query = S[a][:, 0:n * P], qs[:, half, a, t * P:(t + 1) * P]
                    for part in range(2):
                        keys = ks[:, bass.ds((2 * key_head(h, half) + part) * SEQ + lo * P, n * P)]
                        mm = pe.matmul(at, query, keys, start=part == 0, stop=False)
                    if t > 0:
                        mm = pe.matmul(S[a][:, 0:P], eye_b[:], band[:, 0], start=False, stop=t == NC - 1)
                    if t < NC - 1:
                        mm = pe.matmul(S[a][:, (n - 1) * P:n * P], eye_b[:], band[:, 1], start=False, stop=True)
                    mm.then_inc(S[a].full.sem, 1)

            def turns(h, half, t):
                _, n = window(t)
                for a in range(2):
                    use = tile_use(half, t)
                    pe.wait_ge(S[a].free.sem, S[a].free.at(h, tile_use(half, t)))
                    if T[a].free.due(h, use - 1):
                        pe.wait_ge(T[a].free.sem, T[a].free.at(h, use - 1))
                    for j in range(n):
                        mm = pe.transpose(T[a][:, j * P:(j + 1) * P], probs[:, t % 2, a, j * P:(j + 1) * P], eye[:])
                    mm.then_inc(T[a].full.sem, 1)

            def values(h, half, t):
                lo, n = window(t)
                if t == 0:
                    if O.free.due(h, half):
                        pe.wait_ge(O.free.sem, O.free.at(h, half))
                for a in range(2):
                    pe.wait_ge(T[a].free.sem, T[a].free.at(h, tile_use(half, t)))
                    col = (2 * t + a) * HD
                    for j in range(n):
                        mm = pe.matmul(O[:, col:col + HD], probsT[:, t % 2, a, j * P:(j + 1) * P],
                                       v[:, lo + j, bass.ds(key_head(h, half) * HD, HD)], start=j == 0, stop=j == n - 1)
                if t == NC - 1:
                    mm.then_inc(O.full.sem, 1)

            def turn_out(h_before, before, use):
                if W.free.due(h_before + before, use - 1):
                    pe.wait_ge(W.free.sem, W.free.at(h_before + before, use - 1))
                pe.wait_ge(O.free.sem, O.free.at(h_before, before + 1))
                for t in range(NC):
                    mm = pe.transpose(W[:, t * P:(t + 1) * P], normed[:, t * P:(t + 1) * P], eye[:])
                mm.then_inc(W.full.sem, 1)

            def out_tile(h, j, use):
                pe.wait_ge(split.sem, split.at(h, 2))
                pe.wait_ge(o_low.sem, o_low.at(h, 0))
                pe.wait_ge(W.free.sem, W.free.at(h, use - 1))
                for m in range(2):
                    mm = split_product(pe, W[:], o_hi[:, m, j * P:(j + 1) * P], o_lo[:, m, j * P:(j + 1) * P],
                                       y[:, m, 0], y[:, m, 1], m == 0, m == 1)
                mm.then_inc(W.full.sem, 1)

            nrm.sum(pe)
            pe.wait_ge(ready.sem, ready.at(0, 3))
            pe.wait_ge(nrm.logged.sem, nrm.logged.at(0, 1))

            def turn_values(g):
                pe.wait_ge(PB[1].free.sem, PB[1].free.at(0, g - 2))
                if v_kept.due(0, g):
                    pe.wait_ge(v_kept.sem, v_kept.at(0, g))
                for c in range(NC):
                    mm = pe.transpose(T[0][:, c * P:(c + 1) * P], vt[:, c * P:(c + 1) * P], eye[:])
                mm.then_inc(v_turned.sem, 1)

            pe.wait_ge(w_low.sem, w_low.at(0, -4))
            nrm.project(pe, [(w_hi[:, s], w_lo[:, s]) for s in (2, 3)], PB)
            proj(0, -3)
            turn_values(0)
            proj(0, -2)
            proj(0, -1)
            turn_values(1)
            proj(0, 0)
            pe.wait_ge(v_kept.sem, v_kept.at(0, 2))
            pe.wait_ge(k_moved.sem, k_moved.at(0, 8))

            def half_step(h, half, zeroth, last):
                n = 1 if half == 0 else 3
                before, h_before = 1 - half, (h if half else h - 1)
                first, project, outs = zeroth and not half, not (last and half), not zeroth
                if not first:
                    turns(h_before, before, 3)
                scores(h, half, 0)
                if project:
                    proj(h, n, 0)
                if not first:
                    values(h_before, before, 3)
                if project:
                    proj(h, n, 1)
                turns(h, half, 0)
                scores(h, half, 1)
                if project:
                    proj(h, n + 1, 0)
                values(h, half, 0)
                if not first:
                    turn_out(h_before, before, turn_of(half, outs))
                if project:
                    proj(h, n + 1, 1)
                turns(h, half, 1)
                scores(h, half, 2)
                if outs:
                    out_tile(h, 4 * half, 5 * half + 2)
                values(h, half, 1)
                if outs:
                    out_tile(h, 4 * half + 1, 5 * half + 3)
                turns(h, half, 2)
                scores(h, half, 3)
                if outs:
                    out_tile(h, 4 * half + 2, 5 * half + 4)
                values(h, half, 2)
                if outs:
                    out_tile(h, 4 * half + 3, 5 * half + 5)

            def iteration(h, zeroth, last):
                half_step(h, 0, zeroth, last)
                half_step(h, 1, zeroth, last)

            iteration(0, True, False)
            with pe.Fori(1, HEADS - 1) as h:
                iteration(h, False, False)
            iteration(HEADS - 1, False, True)
            turns(HEADS - 1, 1, 3)
            values(HEADS - 1, 1, 3)
            turn_out(HEADS - 1, 1, 1)

            def last_tile(j):
                pe.wait_ge(split.sem, split.at(HEADS, 2))
                pe.wait_ge(w_low.sem, w_low.at(HEADS - 1, 4))
                bank = PB[j % 2]
                pe.wait_ge(bank.free.sem, bank.free.at(HEADS, j // 2 - 1))
                for m in range(2):
                    mm = split_product(pe, bank[:], w_hi[:, 2 + m, j], w_lo[:, 2 + m, j], y[:, m, 0], y[:, m, 1],
                                       m == 0, m == 1)
                mm.then_inc(bank.full.sem, 1)

            def turn_back(t, k):
                bank = row_banks[t][k // 4]
                pe.wait_ge(PB[k % 2].free.sem, PB[k % 2].free.at(HEADS, k // 2))
                if k % 4 == 0:
                    pe.wait_ge(bank.free.sem, bank.free.at(HEADS, {W: 1, PB[0]: 3, PB[1]: 3}.get(bank, 0)))
                mm = pe.transpose(bank[:, (k % 4) * P:(k % 4 + 1) * P], xT[:, k, t * P:(t + 1) * P], eye[:])
                if k % 4 == 3:
                    mm.then_inc(turned_back[k // 4].sem, 1)

            for j in range(KT):
                last_tile(j)
                if 2 <= j < 6:
                    for t in range(NC):
                        turn_back(t, j - 2)
            for t in range(NC):
                for k in range(4, KT):
                    turn_back(t, k)

        @block.scalar
        def _(act):
            act.preload_act_table_set(EXP_LOG)
            def high(h, n):
                s = (n + 3) % SLOTS
                act.wait_ge(w_in_sem[s].sem, w_in_sem[s].at(h, (n + 3) // SLOTS))
                bank, use = bank_of(n - SLOTS)
                if bank.full.due(h, use):
                    act.wait_ge(bank.full.sem, bank.full.at(h, use))
                act.activation(w_hi[:, s], w_raw[:, s], ACT.Copy).then_inc(w_high.sem, 1)

            def high_out(h, m):
                act.wait_ge(o_in.sem, o_in.at(h, m + 1))
                act.wait_ge(W.full.sem, W.full.at(h, 10))
                act.activation(o_hi[:, m], o_raw[:], ACT.Copy).then_inc(o_high.sem, 1)

            def soft_max(h, half, t):
                _, n = window(t)
                act.wait_ge(neg_peak.sem, neg_peak.at(h, tile_use(half, t)))
                for a in range(2):
                    i = 8 * half + 2 * t + a
                    if T[a].full.due(h, tile_use(half, t) - 2):
                        act.wait_ge(T[a].full.sem, T[a].full.at(h, tile_use(half, t) - 2))
                    act.activation(probs[:, t % 2, a, 0:n * P], S[a][:, 0:n * P], ACT.Exp, bias=neg_max[:, i:i + 1],
                                   scale=SCALE, accum_out=row_sum[:, i:i + 1]).then_inc(S[a].free.sem, 1)

            def keep_turn(h, half, t):
                _, n = window(t)
                act.wait_ge(T[0].full.sem, T[0].full.at(h, tile_use(half, t)))
                act.activation(probsT[:, t % 2, 0, 0:n * P], T[0][:, 0:n * P], ACT.Copy).then_inc(T[0].free.sem, 1)

            def exp_sink(h, half):
                act.wait_ge(sink_shift.sem, sink_shift.at(h, half + 1))
                at = weight[:, 8 * half:8 * half + 8]
                act.activation(at, at, ACT.Exp).then_inc(sink_exp.sem, 1)

            def silu(h, n, half, zeroth=False):
                bank, use = bank_of(n)
                act.wait_ge(bank.full.sem, bank.full.at(h, use))
                if not zeroth:
                    if W.free.due(h, turn_of(n // 4, True)):
                        act.wait_ge(W.free.sem, W.free.at(h, turn_of(n // 4, True)))
                act.activation(gate[:, half], bank[:], ACT.Silu).then_inc(bank.free.sem, 1)

            for k in range(KT):
                nrm.square(act, k)
            high(0, -5)
            high(0, -4)
            nrm.root(act)
            high(0, -3)
            nrm.highs(act)
            high(0, -2)
            high(0, -1)

            def take_values(g):
                act.wait_ge(PB[1].full.sem, PB[1].full.at(0, g - 2))
                if v_turned.due(0, g):
                    act.wait_ge(v_turned.sem, v_turned.at(0, g))
                act.activation(vt[:], PB[1][:], ACT.Copy).then_inc(PB[1].free.sem, 1)

            def keep_values(g):
                act.wait_ge(v_turned.sem, v_turned.at(0, g + 1))
                act.activation(v[:, :, g * P:(g + 1) * P], chunked(T[0][:]), ACT.Copy).then_inc(v_kept.sem, 1)

            take_values(0)
            high(0, 0)
            high(0, 1)
            keep_values(0)
            take_values(1)
            high(0, 2)
            keep_values(1)
            silu(0, 0, 0, True)

            def half_step(h, half, zeroth, last):
                before, h_before = 1 - half, (h if half else h - 1)
                n = 3 + 2 * half
                if not (zeroth and not half):
                    keep_turn(h_before, before, 3)
                soft_max(h, half, 0)
                if not zeroth and not half:
                    high_out(h - 1, 0)
                if not last or not half:
                    high(h, n)
                keep_turn(h, half, 0)
                soft_max(h, half, 1)
                if not last or not half:
                    high(h, n + 1)
                if not zeroth and not half:
                    high_out(h - 1, 1)
                keep_turn(h, half, 1)
                soft_max(h, half, 2)
                keep_turn(h, half, 2)
                soft_max(h, half, 3)
                exp_sink(h, half)
                if not (last and half):
                    silu(h, 2 + 2 * half, 1 - half, zeroth and not half)

            def iteration(h, zeroth, last):
                half_step(h, 0, zeroth, last)
                half_step(h, 1, zeroth, last)

            iteration(0, True, False)
            with act.Fori(1, HEADS - 1) as h:
                iteration(h, False, False)
            iteration(HEADS - 1, False, True)
            keep_turn(HEADS - 1, 1, 3)

            for i in range(2):
                for t in range(NC):
                    act.wait_ge(turned_back[i].sem, turned_back[i].at(0, t + 1))
                    act.activation(rows[:, t, i * SEQ:(i + 1) * SEQ], row_banks[t][i][:], ACT.Square,
                                   accum_out=row_squares[:, t, i:i + 1]).then_inc(row_squared.sem, 1)
            act.wait_ge(row_rooted.sem, row_rooted.at(0, 1))
            act.activation(row_rstd[:], row_rstd[:], ACT.Ln, bias=eps, scale=1.0 / DM).then_inc(row_rooted.sem, 1)
            act.wait_ge(row_rooted.sem, row_rooted.at(0, 2))
            act.activation(row_rstd[:], row_rstd[:], ACT.Exp, scale=-0.5).then_inc(row_rooted.sem, 1)

        @block.vector
        def _(dve):
            nrm.add(dve)
            dve.wait_ge(landed.sem, landed.at(0, 3))
            dve.tensor_scalar(neg_sink[:], sink[:], -1.0, None, ALU.mult).then_inc(ready.sem, 1)
            dve.tensor_copy(band[:], band_raw[:]).then_inc(ready.sem, 1)
            dve.tensor_copy(eye_b[:], eye[:]).then_inc(ready.sem, 1)
            dve.wait_ge(ready.sem, ready.at(0, 3))
            nrm.scale(dve)

            def rotate(h, n):
                bank, use = bank_of(n)
                i = {-5: -15, -3: -10, -1: -5, 1: 0, 3: 5}[n]
                dve.wait_ge(bank.full.sem, bank.full.at(h, use))
                if roped.due(h, i):
                    dve.wait_ge(roped.sem, roped.at(h, i))
                dve.tensor_tensor(turned[:, 0], bank[:], rope[:, 0], ALU.mult).then_inc(roped.sem, 1)
                dve.stream_shuffle(turned[:, 1], bank[:], SWAP).then_inc(bank.free.sem, 1)
                dve.wait_ge(bank.free.sem, bank.free.at(h, use))
                dve.tensor_tensor(turned[:, 1], turned[:, 1], rope[:, 1], ALU.mult).then_inc(roped.sem, 1)
                dve.wait_ge(roped.sem, roped.at(h, i + 2))
                dve.tensor_tensor(turned[:, 0], turned[:, 0], turned[:, 1], ALU.add).then_inc(roped.sem, 1)
                dve.wait_ge(roped.sem, roped.at(h, i + 3))
                if n in (-3, -1):
                    dve.wait_ge(k_moved.sem, k_moved.at(0, 2 * n + 10))
                elif n > 0:
                    dve.wait_ge(q_moved.sem, q_moved.at(h, 4 * (n // 2)))
                dve.tensor_copy(parts[:, 0], turned[:, 0]).then_inc(roped.sem, 1)
                dve.wait_ge(roped.sem, roped.at(h, i + 4))
                dve.tensor_tensor(parts[:, 1], turned[:, 0], parts[:, 0].bitcast(F32),
                                  ALU.subtract).then_inc(roped.sem, 1)

            def maxima(h, half, t):
                _, n = window(t)
                i = 8 * half + 2 * t
                for a in range(2):
                    dve.wait_ge(S[a].full.sem, S[a].full.at(h, tile_use(half, t)))
                    dve.tensor_reduce(row_max[:, i + a:i + a + 1], S[a][:, 0:n * P], AX_X,
                                      ALU.max).then_inc(peak.sem, 1)
                dve.wait_ge(peak.sem, peak.at(h, i + 2))
                sinks = neg_sink[:, bass.ds(2 * KT * half + 2 * h, 2)]
                dve.scalar_tensor_tensor(out=neg_max[:, i:i + 2], in0=row_max[:, i:i + 2], scalar=-SCALE, in1=sinks,
                                         op0=ALU.mult, op1=ALU.min).then_inc(neg_peak.sem, 1)

            def keep_turn(h, half, t):
                _, n = window(t)
                dve.wait_ge(T[1].full.sem, T[1].full.at(h, tile_use(half, t)))
                dve.tensor_copy(probsT[:, t % 2, 1, 0:n * P], T[1][:, 0:n * P]).then_inc(T[1].free.sem, 1)

            def shift_sink(h, half):
                dve.wait_ge(neg_peak.sem, neg_peak.at(h, tile_use(half, NC - 1)))
                sinks = sink[:, bass.ds(2 * KT * half + 2 * h, 2)].unsqueeze(1).broadcast_to([P, NC, 2])
                by_tile = lambda ap: ap[:, 8 * half:8 * half + 8].rearrange("p (t a) -> p t a", a=2)
                dve.tensor_tensor(by_tile(weight), by_tile(neg_max), sinks, ALU.add).then_inc(sink_shift.sem, 1)

            def weigh(h, half):
                at = slice(8 * half, 8 * half + 8)
                dve.wait_ge(sink_exp.sem, sink_exp.at(h, half + 1))
                for a in range(2):
                    dve.wait_ge(S[a].free.sem, S[a].free.at(h, tile_use(half, NC - 1)))
                dve.tensor_tensor(weight[:, at], weight[:, at], row_sum[:, at], ALU.add).then_inc(weighed.sem, 1)
                dve.wait_ge(weighed.sem, weighed.at(h, 2 * half + 1))
                dve.reciprocal(weight[:, at], weight[:, at]).then_inc(weighed.sem, 1)

            def normalize(h, half):
                dve.wait_ge(weighed.sem, weighed.at(h, 2 * half + 2))
                dve.wait_ge(O.full.sem, O.full.at(h, half + 1))
                if O.free.due(h, half):
                    dve.wait_ge(O.free.sem, O.free.at(h, half))
                by_head = lambda ap: ap.rearrange("p (g f) -> p g f", f=HD)
                scale = weight[:, 8 * half:8 * half + 8].unsqueeze(2).broadcast_to([P, 8, HD])
                dve.tensor_tensor(by_head(normed[:]), by_head(O[:]), scale, ALU.mult).then_inc(O.free.sem, 1)

            def apply_gate(h, before, use):
                dve.wait_ge(W.full.sem, W.full.at(h, use))
                dve.tensor_tensor(gated[:, before], W[:], gate[:, before], ALU.mult).then_inc(W.free.sem, 1)

            def split_y(h, half, use):
                i = 0 if half else 2
                dve.wait_ge(W.free.sem, W.free.at(h, use))
                dve.wait_ge(W.full.sem, W.full.at(h, 0 if half else 10))
                dve.tensor_copy(y[:, half, 0], gated[:, half]).then_inc(split.sem, 1)
                dve.wait_ge(split.sem, split.at(h, i + 1))
                dve.tensor_tensor(y[:, half, 1], gated[:, half], y[:, half, 0].bitcast(F32),
                                  ALU.subtract).then_inc(split.sem, 1)

            def add_out(h, js, use):
                for j in js:
                    dve.wait_ge(W.full.sem, W.full.at(h, use))
                    dve.wait_ge(W.free.sem, W.free.at(h, use - 1))
                    dve.tensor_tensor(xT[:, j], xT[:, j], W[:], ALU.add).then_inc(W.free.sem, 1)
                    use += 1

            rotate(0, -5)
            rotate(0, -3)
            rotate(0, -1)

            def half_step(h, half, zeroth, last):
                before, h_before = 1 - half, (h if half else h - 1)
                first, use = zeroth and not half, turn_of(half, not zeroth)
                if not first:
                    keep_turn(h_before, before, 3)
                maxima(h, half, 0)
                if not first:
                    weigh(h_before, before)
                    normalize(h_before, before)
                keep_turn(h, half, 0)
                maxima(h, half, 1)
                if not (last and half):
                    rotate(h, 2 * half + 1)
                if not first:
                    apply_gate(h, before, use)
                if not half and not first:
                    split_y(h, 1, use)
                keep_turn(h, half, 1)
                maxima(h, half, 2)
                if not zeroth:
                    add_out(h, range(4 * half, 4 * half + 2), 5 * half + 2)
                keep_turn(h, half, 2)
                maxima(h, half, 3)
                shift_sink(h, half)
                if not zeroth:
                    add_out(h, range(4 * half + 2, 4 * half + 4), 5 * half + 4)
                if half:
                    split_y(h, 0, use)

            def iteration(h, zeroth, last):
                half_step(h, 0, zeroth, last)
                half_step(h, 1, zeroth, last)

            iteration(0, True, False)
            with dve.Fori(1, HEADS - 1) as h:
                iteration(h, False, False)
            iteration(HEADS - 1, False, True)
            keep_turn(HEADS - 1, 1, 3)
            weigh(HEADS - 1, 1)
            normalize(HEADS - 1, 1)
            apply_gate(HEADS, 1, 1)
            split_y(HEADS, 1, 1)
            dve.wait_ge(W.free.sem, W.free.at(HEADS, 1))
            for j in range(KT):
                bank = PB[j % 2]
                dve.wait_ge(bank.full.sem, bank.full.at(HEADS, j // 2))
                dve.tensor_tensor(xT[:, j], xT[:, j], bank[:], ALU.add).then_inc(bank.free.sem, 1)
            dve.wait_ge(row_squared.sem, row_squared.at(0, 2 * NC))
            dve.tensor_tensor(row_rstd[:], row_squares[:, :, 0], row_squares[:, :, 1],
                              ALU.add).then_inc(row_rooted.sem, 1)
            dve.wait_ge(row_rooted.sem, row_rooted.at(0, 3))
            dve.wait_ge(final_landed.sem, final_landed.at(0, 1))
            for t in range(NC):
                for i in range(2):
                    cols = slice(i * SEQ, (i + 1) * SEQ)
                    dve.scalar_tensor_tensor(out=rows[:, t, cols], in0=row_banks[t][i][:], scalar=row_rstd[:, t:t + 1],
                                             in1=w_final[:, cols], op0=ALU.mult, op1=ALU.mult).then_inc(kept.sem, 1)

        @block.gpsimd
        def _(pool):
            def low(h, n):
                s = (n + 3) % SLOTS
                pool.wait_ge(w_high.sem, w_high.at(h, n))
                pool.tensor_tensor(w_lo[:, s], w_raw[:, s], w_hi[:, s].bitcast(F32),
                                   ALU.subtract).then_inc(w_low.sem, 1)

            def low_out(h, m):
                pool.wait_ge(o_high.sem, o_high.at(h, m + 1))
                pool.tensor_tensor(o_lo[:, m], o_raw[:], o_hi[:, m].bitcast(F32),
                                   ALU.subtract).then_inc(o_low.sem, 1)

            for n in range(-5, 3):
                low(0, n)

            def iteration(h, zeroth, last):
                if not zeroth:
                    low_out(h - 1, 0)
                low(h, 3)
                low(h, 4)
                if not zeroth:
                    low_out(h - 1, 1)
                if not last:
                    low(h, 5)
                    low(h, 6)

            iteration(0, True, False)
            with pool.Fori(1, HEADS - 1) as h:
                iteration(h, False, False)
            iteration(HEADS - 1, False, True)


def hybrid_encoder(nc, x, norm_even, w_in_even, lambda_qk, subln_w, hgrn_norm_w, w_out_even, norm_odd, w_in_odd,
                   sink_logits, w_out_odd, final_norm, rope_d, levels_d, eye_d, band_d, out):
    with ExitStack() as ctx:
        sb = lambda name, shape, dt=F32: ctx.enter_context(nc.sbuf_tensor(name, shape, dt))
        xT = sb("xT", [P, KT, SEQ])
        eye, ones, eps = sb("eye", [P, P]), sb("ones", [P, P]), sb("eps", [P, 1])
        rope = sb("rope", [P, 2, SEQ])
        even_layer(nc, xT, eye, ones[:], rope, eps[:], x, w_in_even, w_out_even, norm_even, lambda_qk, subln_w,
                   hgrn_norm_w, rope_d, levels_d, eye_d)
        odd_layer(nc, xT, eye, ones[:], rope, eps[:], w_in_odd, w_out_odd, norm_odd, final_norm, sink_logits,
                  band_d, out)


def constants():
    f32 = np.float32
    inv = f32(500000.0) ** (-np.arange(0, ROPE, 2, dtype=f32) / f32(ROPE))
    ang = np.arange(SEQ, dtype=f32)[None, :] * inv[:, None].astype(f32)
    cos, sin = np.cos(ang).astype(f32), np.sin(ang).astype(f32)
    rope = np.zeros((P, 2, SEQ), f32)
    rope[:, 0] = 1.0
    n = ROPE // 2
    for base in (0, HD):
        rope[base:base + n, 0] = rope[base + n:base + 2 * n, 0] = cos
        rope[base:base + n, 1] = -sin
        rope[base + n:base + 2 * n, 1] = sin
    i = np.arange(P)
    levels = np.stack([(i[:, None] >> l + 1 == i[None, :] >> l + 1) & (i[:, None] >> l != i[None, :] >> l)
                       for l in range(LEVELS)], 1).astype(f32)
    q, k = i[:, None], i[None, :]
    band = np.stack([np.where(k >= q, 0.0, MASKED), np.where(k <= q, 0.0, MASKED)], 1).astype(f32)
    return {"rope": rope, "levels": levels, "eye": np.eye(P, dtype=f32), "band": band}


def kernel(x, norm_even, w_in_even, lambda_qk, subln_w, hgrn_norm_w, hgrn_lb_logits, w_out_even, norm_odd, w_in_odd,
           sink_logits, w_out_odd, final_norm):
    import concourse.bacc as bacc
    from concourse.bass_utils import run_bass_kernel_spmd as run

    x, w_in_even, w_out_even = np.asarray(x), np.asarray(w_in_even), np.asarray(w_out_even)
    assert x.shape == (1, SEQ, DM) and np.asarray(hgrn_lb_logits).shape[1] == 1
    column = lambda a, n: np.ascontiguousarray(np.asarray(a).reshape(n, P).T)
    const = constants()
    arrays = {
        "x": x[0], "norm_even": column(norm_even, KT), "w_in_even": w_in_even[0],
        "lambda_qk": np.asarray(lambda_qk).reshape(1, 4 * HD), "subln_w": column(subln_w, 1),
        "hgrn_norm_w": column(hgrn_norm_w, 1), "w_out_even": w_out_even[0], "norm_odd": column(norm_odd, KT),
        "w_in_odd": np.asarray(w_in_odd)[0], "sink_logits": np.asarray(sink_logits).reshape(1, 2 * PAIRS),
        "w_out_odd": np.asarray(w_out_odd)[0], "final_norm": np.asarray(final_norm).reshape(1, DM),
        "rope": const["rope"], "levels": const["levels"], "eye": const["eye"], "band": const["band"],
    }
    nc = bacc.Bacc("TRN2", target_bir_lowering=False, num_devices=1)
    feeds, args = {}, []
    for name, a in arrays.items():
        feeds[f"in_{name}"] = a = np.ascontiguousarray(a)
        args.append(nc.dram_tensor(f"in_{name}", a.shape, mybir.dt.from_np(a.dtype), kind="ExternalInput").ap())
    args.append(nc.dram_tensor("out", (SEQ, DM), F32, kind="ExternalOutput").ap())
    hybrid_encoder(nc, *args)
    return run(nc, [feeds], core_ids=[0]).results[0]["out"].reshape(1, SEQ, DM)
```
